# Optimizing a Trainium2 kernel written in Bass

```python
import math
import jax, jax.numpy as jnp
from jax import lax
import numpy as np

D_MODEL = 2048
BATCH = 1
SEQ = 256
DEPTH = 1
DEC_BATCH = 8
DEC_SEQ = 8
PAST_LEN = 2048
PAGE_SIZE = 128

N_MEM = 256
GLA_HEADS = 4
GLA_DK = D_MODEL // 2 // GLA_HEADS
GLA_DV = D_MODEL // GLA_HEADS
GLA_RANK = 16
GLA_GATE_NORM = 16.0
HGRN_DK = 128
HGRN_HEADS = D_MODEL // HGRN_DK
HGRN_DV = D_MODEL // HGRN_HEADS
MEM_HEADS = 4
MEM_DH = D_MODEL // MEM_HEADS
D_FF = 5504
CONV_W = 3
CHUNK = 16
EPS = 1e-6

IN_SPLITS = (
    GLA_HEADS * GLA_DK,
    GLA_HEADS * GLA_DK,
    GLA_HEADS * GLA_DV,
    GLA_HEADS * GLA_DV,
    GLA_RANK,
    HGRN_HEADS * HGRN_DK,
    HGRN_HEADS * HGRN_DK,
    HGRN_HEADS * HGRN_DV,
    HGRN_HEADS * HGRN_DV,
    D_MODEL,
    D_MODEL,
)
D_IN = sum(IN_SPLITS)

kernel_name = "gla_hgrn2_gated_merge_memxattn_convffn_step"

def rmsnorm(x, g):
    xf = x.astype(jnp.float32)
    y = xf * lax.rsqrt(jnp.mean(xf * xf, axis=-1, keepdims=True) + EPS)
    return (y * g.astype(jnp.float32)).astype(x.dtype)

def chunked_gated_linear_attention(q, k, v, log_a, s0):
    B, L, H, K = q.shape
    V = v.shape[-1]
    C = math.gcd(CHUNK, L)
    N = L // C

    def to_chunks(t):
        return t.astype(jnp.float32).reshape(B, N, C, H, t.shape[-1]).transpose(1, 0, 3, 2, 4)

    qc, kc, vc, ac = to_chunks(q), to_chunks(k), to_chunks(v), to_chunks(log_a)
    causal = jnp.tril(jnp.ones((C, C), dtype=bool))

    def step(S, xs):
        qn, kn, vn, an = xs
        b = jnp.cumsum(an, axis=-2)
        b_last = b[..., -1:, :]
        q_dec = qn * jnp.exp(b)
        k_inv = kn * jnp.exp(-b)
        k_end = kn * jnp.exp(b_last - b)
        scores = jnp.where(causal, jnp.einsum('bhck,bhsk->bhcs', q_dec, k_inv), 0.0)
        o = jnp.einsum('bhcs,bhsv->bhcv', scores, vn) + jnp.einsum('bhck,bhkv->bhcv', q_dec, S)
        S = jnp.exp(b_last[..., 0, :])[..., None] * S + jnp.einsum('bhsk,bhsv->bhkv', k_end, vn)
        return S, o

    s_final, o = lax.scan(step, s0.astype(jnp.float32), (qc, kc, vc, ac))
    o = o.transpose(1, 0, 3, 2, 4).reshape(B, L, H, V)
    return o.astype(v.dtype), s_final.astype(s0.dtype)

def head_gated_norm(o, g_norm, gate):
    B, L, H, V = o.shape
    return rmsnorm(o, g_norm.reshape(H, V)).reshape(B, L, H * V) * jax.nn.silu(gate)

def memory_kv(mem, norm_mem_g, w_mem_k, w_mem_v):
    B, M, _ = mem.shape
    hm = rmsnorm(mem, norm_mem_g)
    return (hm @ w_mem_k).reshape(B, M, MEM_HEADS, MEM_DH), (hm @ w_mem_v).reshape(B, M, MEM_HEADS, MEM_DH)

def hybrid_layer(x, mem_k, mem_v, s_gla, s_hgrn, conv_buf, lb, p):
    B, L, _ = x.shape
    h = rmsnorm(x, p['norm_mix_g'])
    z = h @ p['w_in']
    offsets = np.cumsum(IN_SPLITS)[:-1].tolist()
    gq, gk, gv, gg, ga, hq, hf, hi, hg, mix_a, mix_b = jnp.split(z, offsets, axis=-1)
    gla_q = gq.reshape(B, L, GLA_HEADS, GLA_DK) * (GLA_DK ** -0.5)
    gla_k = gk.reshape(B, L, GLA_HEADS, GLA_DK)
    gla_v = gv.reshape(B, L, GLA_HEADS, GLA_DV)
    a_logit = (ga @ p['gla_w_a_up'] + p['gla_b_a']).astype(jnp.float32)
    gla_log_a = (jax.nn.log_sigmoid(a_logit) / GLA_GATE_NORM).reshape(B, L, GLA_HEADS, GLA_DK)
    o_gla, s_gla_new = chunked_gated_linear_attention(gla_q, gla_k, gla_v, gla_log_a, s_gla)
    o_gla = head_gated_norm(o_gla, p['gla_norm_g'], gg)
    f = lb + (1.0 - lb) * jax.nn.sigmoid(hf.astype(jnp.float32))
    h_k = (1.0 - f).reshape(B, L, HGRN_HEADS, HGRN_DK)
    h_log_f = jnp.log(f).reshape(B, L, HGRN_HEADS, HGRN_DK)
    h_q = jax.nn.silu(hq).reshape(B, L, HGRN_HEADS, HGRN_DK) * (HGRN_DK ** -0.5)
    h_i = hi.reshape(B, L, HGRN_HEADS, HGRN_DV)
    o_hgrn, s_hgrn_new = chunked_gated_linear_attention(h_q, h_k, h_i, h_log_f, s_hgrn)
    o_hgrn = head_gated_norm(o_hgrn, p['hgrn_norm_g'], hg)
    o_mix = jax.nn.sigmoid(mix_a) * o_gla + jax.nn.sigmoid(mix_b) * o_hgrn
    x = x + (o_mix @ p['w_out']).astype(x.dtype)
    hx = rmsnorm(x, p['norm_xattn_g'])
    mq = (hx @ p['w_mem_q']).reshape(B, L, MEM_HEADS, MEM_DH)
    sc = jnp.einsum('blhd,bmhd->bhlm', mq, mem_k).astype(jnp.float32) * (MEM_DH ** -0.5)
    pr = jax.nn.softmax(sc, axis=-1).astype(mem_v.dtype)
    mo = jnp.einsum('bhlm,bmhd->blhd', pr, mem_v).reshape(B, L, D_MODEL)
    x = x + (mo @ p['w_mem_o']).astype(x.dtype)
    hf_ = rmsnorm(x, p['norm_ffn_g'])
    u = hf_ @ p['w_ffn_up']
    ug, uv = u[..., :D_FF], u[..., D_FF:]
    seq = jnp.concatenate([conv_buf.astype(ug.dtype), ug], axis=1)
    w = p['ffn_conv_w']
    conv = sum(w[j] * seq[:, j:j + L] for j in range(CONV_W)) + p['ffn_conv_b']
    act = jax.nn.silu(conv) * uv
    x = x + (act @ p['w_ffn_down']).astype(x.dtype)
    conv_new = seq[:, -(CONV_W - 1):].astype(conv_buf.dtype)
    return x, s_gla_new, s_hgrn_new, conv_new

def setup_inputs(seed: int = 0) -> dict:
    key = jax.random.key(seed)
    ks = jax.random.split(key, 32)
    f32 = jnp.float32

    def nrm(k, shape, scale):
        return jax.random.normal(k, shape, f32) * scale

    def gain(k, shape):
        return 1.0 + 0.02 * jax.random.normal(k, shape, f32)

    return {
        "x_prompt": nrm(ks[0], (BATCH, SEQ, D_MODEL), 1.0),
        "x_sample": nrm(ks[1], (DEC_BATCH, DEC_SEQ, D_MODEL), 1.0),
        "mem_prompt": nrm(ks[2], (BATCH, N_MEM, D_MODEL), 1.0),
        "state_gla": nrm(ks[3], (DEPTH, DEC_BATCH, GLA_HEADS, GLA_DK, GLA_DV), 0.3),
        "state_hgrn": nrm(ks[4], (DEPTH, DEC_BATCH, HGRN_HEADS, HGRN_DK, HGRN_DV), 0.3),
        "state_ffn_conv": nrm(ks[5], (DEPTH, DEC_BATCH, CONV_W - 1, D_FF), 1.0),
        "cache_mem_k": nrm(ks[6], (DEPTH, DEC_BATCH, N_MEM, MEM_HEADS, MEM_DH), 1.0),
        "cache_mem_v": nrm(ks[7], (DEPTH, DEC_BATCH, N_MEM, MEM_HEADS, MEM_DH), 1.0),
        "norm_mix_g": gain(ks[8], (DEPTH, D_MODEL)),
        "w_in": nrm(ks[9], (DEPTH, D_MODEL, D_IN), D_MODEL ** -0.5),
        "gla_w_a_up": nrm(ks[10], (DEPTH, GLA_RANK, GLA_HEADS * GLA_DK), GLA_RANK ** -0.5),
        "gla_b_a": nrm(ks[11], (DEPTH, GLA_HEADS * GLA_DK), 0.1),
        "gla_norm_g": gain(ks[12], (DEPTH, GLA_HEADS * GLA_DV)),
        "hgrn_lower_bound": nrm(ks[13], (DEPTH + 1, HGRN_HEADS * HGRN_DK), 0.1),
        "hgrn_norm_g": gain(ks[14], (DEPTH, HGRN_HEADS * HGRN_DV)),
        "w_out": nrm(ks[15], (DEPTH, D_MODEL, D_MODEL), D_MODEL ** -0.5),
        "norm_xattn_g": gain(ks[16], (DEPTH, D_MODEL)),
        "norm_mem_g": gain(ks[17], (DEPTH, D_MODEL)),
        "w_mem_q": nrm(ks[18], (DEPTH, D_MODEL, D_MODEL), D_MODEL ** -0.5),
        "w_mem_k": nrm(ks[19], (DEPTH, D_MODEL, D_MODEL), D_MODEL ** -0.5),
        "w_mem_v": nrm(ks[20], (DEPTH, D_MODEL, D_MODEL), D_MODEL ** -0.5),
        "w_mem_o": nrm(ks[21], (DEPTH, D_MODEL, D_MODEL), D_MODEL ** -0.5),
        "norm_ffn_g": gain(ks[22], (DEPTH, D_MODEL)),
        "w_ffn_up": nrm(ks[23], (DEPTH, D_MODEL, 2 * D_FF), D_MODEL ** -0.5),
        "ffn_conv_w": nrm(ks[24], (DEPTH, CONV_W, D_FF), CONV_W ** -0.5),
        "ffn_conv_b": nrm(ks[25], (DEPTH, D_FF), 0.02),
        "w_ffn_down": nrm(ks[26], (DEPTH, D_FF, D_MODEL), D_FF ** -0.5),
        "norm_final_g": gain(ks[27], (D_MODEL,)),
    }

def reference(x_prompt, x_sample, mem_prompt, state_gla, state_hgrn, state_ffn_conv, cache_mem_k, cache_mem_v,
              norm_mix_g, w_in, gla_w_a_up, gla_b_a, gla_norm_g, hgrn_lower_bound, hgrn_norm_g, w_out,
              norm_xattn_g, norm_mem_g, w_mem_q, w_mem_k, w_mem_v, w_mem_o,
              norm_ffn_g, w_ffn_up, ffn_conv_w, ffn_conv_b, w_ffn_down, norm_final_g):
    lb_all = jnp.cumsum(jax.nn.softmax(hgrn_lower_bound.astype(jnp.float32), axis=0), axis=0)
    xp, xs = x_prompt, x_sample
    Bp = x_prompt.shape[0]
    gla_p, hgrn_p, conv_p, mk_p, mv_p = [], [], [], [], []
    gla_s, hgrn_s, conv_s = [], [], []
    for l in range(DEPTH):
        p = {
            'norm_mix_g': norm_mix_g[l], 'w_in': w_in[l], 'gla_w_a_up': gla_w_a_up[l], 'gla_b_a': gla_b_a[l],
            'gla_norm_g': gla_norm_g[l], 'hgrn_norm_g': hgrn_norm_g[l], 'w_out': w_out[l],
            'norm_xattn_g': norm_xattn_g[l], 'w_mem_q': w_mem_q[l], 'w_mem_o': w_mem_o[l],
            'norm_ffn_g': norm_ffn_g[l], 'w_ffn_up': w_ffn_up[l], 'ffn_conv_w': ffn_conv_w[l],
            'ffn_conv_b': ffn_conv_b[l], 'w_ffn_down': w_ffn_down[l],
        }
        lb = lb_all[l]
        mk, mv = memory_kv(mem_prompt, norm_mem_g[l], w_mem_k[l], w_mem_v[l])
        s0_gla = jnp.zeros((Bp, GLA_HEADS, GLA_DK, GLA_DV), x_prompt.dtype)
        s0_hgrn = jnp.zeros((Bp, HGRN_HEADS, HGRN_DK, HGRN_DV), x_prompt.dtype)
        c0 = jnp.zeros((Bp, CONV_W - 1, D_FF), x_prompt.dtype)
        xp, sg, sh, cb = hybrid_layer(xp, mk, mv, s0_gla, s0_hgrn, c0, lb, p)
        gla_p.append(sg); hgrn_p.append(sh); conv_p.append(cb); mk_p.append(mk); mv_p.append(mv)
        xs, sg2, sh2, cb2 = hybrid_layer(xs, cache_mem_k[l], cache_mem_v[l], state_gla[l], state_hgrn[l],
                                         state_ffn_conv[l], lb, p)
        gla_s.append(sg2); hgrn_s.append(sh2); conv_s.append(cb2)
    y_prompt = rmsnorm(xp, norm_final_g)
    y_sample = rmsnorm(xs, norm_final_g)
    new_gla_prompt = jnp.stack(gla_p)
    new_hgrn_prompt = jnp.stack(hgrn_p)
    new_conv_prompt = jnp.stack(conv_p)
    new_mem_k_prompt = jnp.stack(mk_p)
    new_mem_v_prompt = jnp.stack(mv_p)
    new_gla_sample = jnp.stack(gla_s)
    new_hgrn_sample = jnp.stack(hgrn_s)
    new_conv_sample = jnp.stack(conv_s)
    return (y_prompt, y_sample, new_gla_prompt, new_hgrn_prompt, new_conv_prompt, new_mem_k_prompt,
            new_mem_v_prompt, new_gla_sample, new_hgrn_sample, new_conv_sample)


_drawn_inputs = setup_inputs


def setup_inputs(seed=0):
    import zlib

    import numpy as np

    out = dict(_drawn_inputs(seed))
    spreads = {}
    factors = {'gla_norm_g': 8.0,
     'hgrn_norm_g': 8.0,
     'norm_xattn_g': 8.0,
     'norm_mem_g': 2.824,
     'norm_ffn_g': 2.833,
     'ffn_conv_b': 5.876,
     'norm_final_g': 2.826}
    for name, (base, spread) in spreads.items():
        noise = np.random.default_rng([zlib.crc32(name.encode()), seed]).standard_normal(out[name].shape)
        drawn = base * np.exp(spread * noise) if base else spread * noise
        out[name] = __import__('jax').numpy.asarray(drawn.astype(out[name].dtype))
    for name, factor in factors.items():
        out[name] = (out[name] * factor).astype(out[name].dtype)
    return out
```

```python
from contextlib import ExitStack, contextmanager

import concourse.bass as bass
from concourse import mybir

F32 = mybir.dt.float32
F32R = mybir.dt.float32r
U32 = mybir.dt.uint32
ALU = mybir.AluOpType
ACT = mybir.ActivationFunctionType
AX = mybir.AxisListType
ds = bass.ds

P = 128
D = 2048
KT = D // P
NP, B, L = 256, 8, 8
NS = B * L
NT = NP + NS
M = 256
FF = 5504
FT = FF // P
GH, GK, GV = 4, 256, 512
HH = 16
MH, MD = 4, 512
C = 32
NC = NP // C
CPB = P // C
EPS = 1e-6
NSEQ = NP + 2 + B * (L + 2)
NCONV = NSEQ - 2

ARENA = 96 * 1024 + 256
GROUPS = ((0, 16), (16, 16), (32, FT - 32))
CPART = 24
GQ, GKC = 0, GH * GK
GVC = GKC + GH * GK
GG = GVC + GH * GV
GA = GG + GH * GV
HQ = GA + 16
HF, HI, HG = HQ + D, HQ + 2 * D, HQ + 3 * D
MA, MB = HQ + 4 * D, HQ + 5 * D

PAR = {}
_at = 0
for _name, _rows in (("mix", KT), ("ba", 8), ("glan", KT), ("lb0", KT), ("lb1", KT), ("hgn", KT), ("xat", KT), ("mem", KT),
                     ("ffn", KT), ("fin", KT), ("cw0", FT), ("cw1", FT), ("cw2", FT), ("cb", FT)):
    if _at // P != (_at + _rows - 1) // P:
        _at = (_at // P + 1) * P
    PAR[_name] = (_at, _rows)
    _at += _rows
PBLK = (_at + P - 1) // P

PER = {('act', 'down0'): {'ahead': 4, 'tile': 4},
 ('act', 'down1'): {'ahead': 4, 'tile': 4},
 ('act', 'down2'): {'ahead': 4, 'tile': 4},
 ('act', 'gla'): {'ahead': 16,
                  'alog': 2,
                  'decay': 1,
                  'inter': 7,
                  'mix': 1,
                  'o': 1,
                  'root': 1,
                  'step': 2,
                  'tile': 16,
                  'turned': 6},
 ('act', 'hgrn'): {'ahead': 20,
                   'decay': 2,
                   'f': 2,
                   'mix': 2,
                   'o': 2,
                   'o_copied': 4,
                   'root': 2,
                   'step': 2,
                   'tile': 20,
                   'turned': 8},
 ('act', 'mem_k1'): {'ahead': 4, 'memo0': 1, 'memo1': 1, 'memturn': 4, 'tile': 4},
 ('act', 'mem_v'): {'ahead': 4, 'memo0': 1, 'memo1': 1, 'memturn': 4, 'tile': 4},
 ('act', 'memo'): {'ahead': 4, 'tile': 4},
 ('act', 'memq'): {'ahead': 4, 'tile': 4},
 ('act', 'up0'): {'ahead': 4, 'conv': 2, 'tile': 4},
 ('act', 'up1'): {'ahead': 4, 'conv': 2, 'tile': 4},
 ('act', 'up2'): {'ahead': 4, 'conv': 2, 'tile': 4},
 ('act', 'wout'): {'ahead': 4, 'tile': 4},
 ('act', 'xattn'): {'kturn': 8, 'smp': 1, 'v_used': 4},
 ('dve', 'down0'): {'tile': 4},
 ('dve', 'down1'): {'tile': 4},
 ('dve', 'down2'): {'sqr': 4, 'step': 4, 'tile': 4},
 ('dve', 'gla'): {'abs': 2,
                  'exps': 1,
                  'gate': 8,
                  'inter': 7,
                  'kv': 32,
                  'ln': 1,
                  'mixed': 1,
                  'pstate': 1,
                  'root': 1,
                  'sample_ready': 16,
                  'scores': 1,
                  'ss': 1,
                  'st': 16,
                  'step': 33,
                  'tile': 16,
                  'turned': 6},
 ('dve', 'hgrn'): {'exps': 2,
                   'f_exp': 4,
                   'f_ready': 2,
                   'gate': 12,
                   'inter': 14,
                   'kv': 64,
                   'ln': 2,
                   'mixed': 2,
                   'pstate': 2,
                   'root': 2,
                   'sample_ready': 32,
                   'scores': 2,
                   'ss': 2,
                   'st': 32,
                   'step': 62,
                   'tile': 20,
                   'turned': 8},
 ('dve', 'memo'): {'sqr': 4, 'step': 4, 'tile': 4},
 ('dve', 'up0'): {'conv': 4, 'step': 31, 'tile': 8},
 ('dve', 'up1'): {'conv': 4, 'step': 31, 'tile': 8},
 ('dve', 'up2'): {'conv': 4, 'step': 31, 'tile': 8},
 ('dve', 'wout'): {'sqr': 4, 'step': 8, 'tile': 4},
 ('dve', 'xattn'): {'kturn': 8, 'smp': 1, 'step': 2},
 ('pe', 'down0'): {'tile': 4},
 ('pe', 'down1'): {'tile': 4},
 ('pe', 'down2'): {'tile': 4},
 ('pe', 'gla'): {'o': 3,
                 'prep': 1,
                 's0_in0': 2,
                 's0_in1': 2,
                 's0_in2': 2,
                 's0_in3': 2,
                 'sample_ready': 16,
                 'ss': 1,
                 'state_ready': 16,
                 'tile': 16,
                 'turned': 6,
                 'wa': 1},
 ('pe', 'hgrn'): {'o': 4,
                  'pair': 2,
                  'prep': 2,
                  's0_in0': 2,
                  's0_in1': 2,
                  'sample_ready': 32,
                  'ss': 2,
                  'state_ready': 32,
                  'tile': 20,
                  'turned': 8},
 ('pe', 'mem_k'): {'memturn': 4, 'tile': 4},
 ('pe', 'mem_v'): {'memturn': 4, 'tile': 4},
 ('pe', 'memo'): {'tile': 4},
 ('pe', 'memq'): {'tile': 4},
 ('pe', 'up0'): {'tile': 4},
 ('pe', 'up1'): {'tile': 4},
 ('pe', 'up2'): {'tile': 4},
 ('pe', 'wout'): {'tile': 4, 'xst': 4},
 ('pe', 'xattn'): {'kc0': 1, 'kc1': 1, 'kc2': 1, 'kc3': 1, 'kturn': 8, 'smp': 1, 'vc0': 1, 'vc1': 1, 'vc2': 1, 'vc3': 1},
 ('pool', 'split'): {'tile': 4},
 ('sp', 'down0'): {'load': 2},
 ('sp', 'down1'): {'load': 2},
 ('sp', 'down2'): {'load': 2},
 ('sp', 'gla'): {'load': 8,
                 's0_out0': 2,
                 's0_out1': 2,
                 's0_out2': 2,
                 's0_out3': 2,
                 'sample_ready': 16,
                 'state_ready': 16,
                 'wa': 1},
 ('sp', 'hgrn'): {'load': 10, 's0_out0': 2, 's0_out1': 2, 'sample_ready': 32, 'state_ready': 32},
 ('sp', 'mem_k'): {'load': 2},
 ('sp', 'mem_v'): {'load': 2},
 ('sp', 'memo'): {'load': 2},
 ('sp', 'memq'): {'load': 2},
 ('sp', 'up0'): {'load': 2},
 ('sp', 'up1'): {'load': 2},
 ('sp', 'up2'): {'load': 2},
 ('sp', 'wout'): {'load': 2},
 ('sp', 'xattn'): {'k_turned': 8, 'v_used': 4}}
RECORD = None


class Counts:

    def __init__(self, who):
        self.who, self.n, self.per, self.i = who, {}, {}, None

    def add(self, name, k=1):
        self.n[name] = self.n.get(name, 0) + k

    def now(self, name, lag=0, unit=1):
        n, per = self.n.get(name, 0) - lag, self.per.get(name, 0)
        if self.i is None or not per:
            return n * unit
        assert n >= 0, (self.who, name, n)
        return self.i * (per * unit) + n * unit

    def next(self, name, unit=1):
        self.add(name)
        return self.now(name, 0, unit)

    def slot(self, name, k):
        assert self.per.get(name, 0) % k == 0, (self.who, name, self.per.get(name), k)
        return self.n.get(name, 0) % k

    def rounds(self, name, k, lag=0, unit=1, more=0):
        n, per = (self.n.get(name, 0) - lag) // k + more, self.per.get(name, 0) // k
        if self.i is None or not per:
            return n * unit
        assert n >= 0, (self.who, name, n)
        return self.i * (per * unit) + n * unit

    @contextmanager
    def turns(self, eng, name, n):
        per = PER.get((self.who, name), {})
        start = dict(self.n)
        with eng.Fori(0, n) as i:
            self.i, self.per = i, per
            yield i
            grown = {k: v - start.get(k, 0) for k, v in self.n.items() if v != start.get(k, 0)}
            if RECORD is not None:
                RECORD[self.who, name] = grown
            else:
                assert grown == per, (self.who, name, grown, per)
        self.i, self.per = None, {}
        self.n = {k: start.get(k, 0) + grown.get(k, 0) * n for k in self.n}


def wait(eng, sem, value):
    if not (isinstance(value, int) and value <= 0):
        eng.wait_ge(sem, value)


def build(nc, a, out):
    ctx = ExitStack()
    with ctx:
        sems = {}

        class Sems:
            def __getattribute__(self, name):
                if name not in sems:
                    sems[name] = ctx.enter_context(nc.semaphore(name))
                return sems[name]
        S = Sems()

        def sb(name, shape, dt=F32):
            return ctx.enter_context(nc.sbuf_tensor(name, shape, dt))

        raw = [sb(f"raw{s}", [P, KT, 2 * P]) for s in range(2)]
        wH = [sb(f"wH{s}", [P, KT, P], F32R) for s in range(2)]
        wL = [sb(f"wL{s}", [P, KT, P], F32R) for s in range(2)]
        hH = sb("hH", [P, KT, NT], F32R)
        hL = sb("hL", [P, KT, NT], F32R)
        ident = sb("ident", [P, P])
        ones = sb("ones", [P, P])
        causal = sb("causal", [P, P])
        causal8 = sb("causal8", [NS, NS])
        own8 = sb("own8", [NS, B])
        keep = sb("keep", [P, NT])
        par = sb("par", [P, PBLK, P])
        lb = sb("lb", [P, KT])
        oml = sb("oml", [P, KT])
        small = sb("small", [P, 64])
        wah = sb("wah", [16, GK])
        gaT = sb("gaT", [16, NT])

        base = nc.sbuf_base
        sb("arena", [P, ARENA // 4])

        def at(name, kb, shape, dt=F32):
            n = 4
            for s in shape[1:]:
                n *= s
            assert kb * 1024 + n <= ARENA, (name, kb * 1024 + n)
            return nc.alloc_sbuf_tensor_at(name, shape, dt, offset=base + int(kb * 1024))

        mtok = at("mtok", 0, [P, 2, D])
        xtok = at("xtok", 16, [P, 3, D])
        mH = at("mH", 40, [P, KT, M], F32R)
        mL = at("mL", 56, [P, KT, M], F32R)
        sqtok = at("sqtok", 72, [P, D])
        memo = [at(f"memo{s}", 80 + 2 * s, [P, 2, 2 * P]) for s in range(2)]
        memf = [at(f"memf{s}", 86 + s, [P, M]) for s in range(2)]
        parrow = at("parrow", 84, [P, PBLK, P])
        omix = at("omix", 0, [P, KT, NT])
        s0g = [at(f"s0g{s}", 20 + 4 * s, [P, 2, GV]) for s in range(4)]
        s0h = [at(f"s0h{s}", 20 + 8 * s, [P, B, 2, P]) for s in range(2)]
        qd = at("qd", 36, [P, 2, NT])
        ki = at("ki", 38.5, [P, 2, NT])
        cum = at("cum", 41, [P, 2, NT])
        cmid = at("cmid", 43.5, [P, 2, NT])
        e1 = at("e1", 46, [P, 2, NT])
        e2 = at("e2", 48.5, [P, 2, NT])
        ke = at("ke", 51, [P, 2, NT])
        qi = at("qi", 53.5, [P, 2, NP])
        vo = at("vo", 55.5, [P, 4, NT])
        vtok = at("vtok", 60.5, [P, 3, GV])
        ktok = at("ktok", 66.5, [P, 3, 2 * P])
        kmask = at("kmask", 69.5, [NS, B, 2 * P])
        sp = [at(f"sp{s}", 77.5 + 4 * s, [P, 2, GV]) for s in range(2)]
        gate = at("gate", 85.5, [P, 4, NT])
        ge = [at(f"ge{s}", 90.5 + 1.25 * s, [P, NT]) for s in range(2)]
        bd = at("bd", 93, [P, 2, NP])
        bds = at("bds", 95, [NS, 2, NS])
        emid = at("emid", 95.5, [P, 2, NC])
        elast = at("elast", 95.5625, [P, 2, NC])
        sqg = at("sqg", 41, [P, 4, NT])
        rsg = at("rsg", 46, [P, 2, NT])
        tmpg = at("tmpg", 48.5, [P, 2, NT])
        x = at("x", 0, [P, KT, NT])
        xres = at("xres", 20, [P, 3, D])
        xst = [at(f"xst{s}", 44 + 1.5 * s, [P, 3, P]) for s in range(2)]
        q = at("q", 20, [P, KT, NT])
        nrm = [at(f"nrm{s}", 20 + 5 * s, [P, 4, NT]) for s in range(2)]
        kc = at("kc", 44, [P, MH, 2, MD])
        vc = at("vc", 60, [P, MH, 2, MD])
        kT = at("kT", 76, [P, MH, 4, M])
        acc = at("acc", 92, [P, NT])
        sq = [at(f"sq{s}", 93.25 + 1.25 * s, [P, NT]) for s in range(2)]
        rs = at("rs", 40, [P, NT])
        sTs = at("sTs", 92, [P, 64])
        pr = at("pr", 92.25, [32, M])
        pTs = at("pTs", 93.25, [P, 2, 32])
        pP = at("pP", 41.5, [P, 2, M])
        pTP = at("pTP", 93.5, [P, 2, NP])
        aH = at("aH", 20, [P, KT, NT], F32R)
        aL = at("aL", 41.5, [P, KT, NT], F32R)
        crow = at("crow", 62, [18, CPART * P])
        crow1 = at("crow1", 41.5, [16, (FT - CPART) * P])
        cin = at("cin", 74, [P, FT, 16])
        cnew = at("cnew", 76.75, [P, FT, 18])
        seq = [at(f"seq{s}", 80 + 1.375 * s, [P, NSEQ]) for s in range(2)]
        cv = [at(f"cv{s}", 82.75 + 1.375 * s, [P, NSEQ]) for s in range(2)]
        ce = [at(f"ce{s}", 85.5 + 1.375 * s, [P, NSEQ]) for s in range(2)]
        av = [at(f"av{s}", 88.25 + 1.25 * s, [P, NT]) for s in range(2)]
        ytok = at("ytok", 42, [P, 3, D])

        ps = [ctx.enter_context(nc.psum_tensor(n, [P, 512], F32)) for n in ("P0", "P1", "T0", "T1", "O0", "O1", "KV0", "KV1")]
        PB, T, O, KV = ps[0:2], ps[2:4], ps[4:6], ps[6:8]
        RB = [O[0], O[1], KV[0], KV[1]]

        def pcol(name, t, n=1):
            at0, rows = PAR[name]
            return par[:, at0 // P, ds(at0 % P + t, n)]

        landed = [S.landed0, S.landed1]
        bank_free = [S.bank0_free, S.bank1_free]
        high_ready, low_ready, tile_done = S.high_ready, S.low_ready, S.tile_done
        mem_out = [S.mem_out0, S.mem_out1]
        s0_in = [S.s0_in0, S.s0_in1, S.s0_in2, S.s0_in3]
        s0_out = [S.s0_out0, S.s0_out1, S.s0_out2, S.s0_out3]
        kc_in = [S.kc_in0, S.kc_in1, S.kc_in2, S.kc_in3]
        vc_in = [S.vc_in0, S.vc_in1, S.vc_in2, S.vc_in3]

        w_in = a["w_in"][0]
        w_up = a["w_ffn_up"][0]
        rows_of = lambda ap: ap.rearrange("(t p) n -> p t n", p=P)
        NLOADS = 16 + 1 + 32 + 40 + 8 + 8 + 8 + FT + 24
        NTILES = 2 * NLOADS
        mk_out = out["mem_k"][0, 0].rearrange("(t p) h d -> p t (h d)", p=P)
        mv_out = out["mem_v"][0, 0].rearrange("(t p) h d -> p t (h d)", p=P)

        block = ctx.enter_context(nc.Block())

        @block.sync
        def _(sp_):
            k = Counts("sp")

            def begin_load():
                s = k.slot("load", 2)
                wait(sp_, low_ready, k.now("load", 1, 2))
                k.add("load")
                return s

            def load(w, col, nk=KT):
                s = begin_load()
                half = (nk + 1) // 2
                for lo, hi in ((0, half), (half, nk)):
                    sp_.dma_start(raw[s][:, lo:hi, :], rows_of(w)[:, lo:hi, ds(col, 2 * P)]).then_inc(landed[s], 16)

            sp_.dma_start(mtok[:], a["mem_prompt"][0].rearrange("(b p) d -> p b d", p=P)).then_inc(S.mem_in, 16)
            names = {"mix": a["norm_mix_g"][0], "ba": a["gla_b_a"][0], "glan": a["gla_norm_g"][0],
                     "lb0": a["hgrn_lower_bound"][0], "lb1": a["hgrn_lower_bound"][1], "hgn": a["hgrn_norm_g"][0],
                     "xat": a["norm_xattn_g"][0], "mem": a["norm_mem_g"][0], "ffn": a["norm_ffn_g"][0],
                     "fin": a["norm_final_g"], "cw0": a["ffn_conv_w"][0, 0], "cw1": a["ffn_conv_w"][0, 1],
                     "cw2": a["ffn_conv_w"][0, 2], "cb": a["ffn_conv_b"][0]}
            wait(sp_, S.rows_cleared, 1)
            for n, src in names.items():
                r0, rows = PAR[n]
                sp_.dma_start(parrow[r0 % P:r0 % P + rows, r0 // P, :], src.rearrange("(t p) -> t p", p=P)).then_inc(S.par_in, 16)
            load(a["w_mem_k"][0], 0)
            load(a["w_mem_k"][0], 2 * P)
            sp_.dma_start(xtok[:, 0:2, :], a["x_prompt"][0].rearrange("(b p) d -> p b d", p=P)).then_inc(S.x_in, 16)
            sp_.dma_start(xtok[0:NS, 2, :], a["x_sample"].rearrange("b l d -> (b l) d")).then_inc(S.x_in, 16)
            with k.turns(sp_, "mem_k", 3) as i:
                for s in range(2):
                    load(a["w_mem_k"][0], i * (4 * P) + (2 + s) * 2 * P)
            with k.turns(sp_, "mem_v", 4) as i:
                for s in range(2):
                    load(a["w_mem_v"][0], i * (4 * P) + s * 2 * P)
            load(w_in, GA)
            sg = a["state_gla"][0]

            def s0_load(b, h):
                s = b % 4
                wait(sp_, s0_out[s], k.now(f"s0_out{s}", 0, 16))
                sp_.dma_start(s0g[s][:], sg[b, ds(h, 1)].rearrange("o (t p) v -> p (o t) v", p=P)).then_inc(s0_in[s], 16)

            def s0_store(b, h):
                s = b % 4
                k.add("sample_ready", 2)
                wait(sp_, S.sample_ready, k.now("sample_ready"))
                sp_.dma_start(out["gla_s"][0, b, ds(h, 1)].rearrange("o (t p) v -> p (o t) v", p=P), s0g[s][:]).then_inc(s0_out[s], 16)
                k.add(f"s0_out{s}")

            def gla_head(h, after):
                load(w_in, h * GV + GVC)
                load(w_in, h * GV + GVC + 2 * P)
                for b in range(4):
                    if b == 0:
                        wait(sp_, tile_done, 32)
                    s0_load(b, h)
                for g in (GG, MA):
                    load(w_in, h * GV + g)
                    load(w_in, h * GV + g + 2 * P)
                for b in range(4):
                    s0_store(b, h)
                for b in range(4, 8):
                    s0_load(b, h)
                after()
                for b in range(4, 8):
                    s0_store(b, h)
                k.add("state_ready", 2 * NC)
                wait(sp_, S.state_ready, k.now("state_ready"))
                sp_.dma_start(out["gla_p"][0, 0, ds(h, 1)].rearrange("o (t p) v -> p (o t) v", p=P), sp[0][:]).then_inc(S.pstate_out, 16)

            def gla_qk(h):
                wait(sp_, S.alog_done, k.now("wa", 0, 2))
                sp_.dma_start(wah[:], a["gla_w_a_up"][0][:, ds(h * GK, GK)]).then_inc(S.wa_in, 16)
                k.add("wa")
                load(w_in, h * GK + GQ)
                load(w_in, h * GK + GKC)

            gla_qk(0)
            with k.turns(sp_, "gla", GH - 1) as h:
                gla_head(h, lambda: gla_qk(h + 1))

            sh = a["state_hgrn"][0]

            def hgrn_fq(p):
                load(w_in, p * (2 * P) + HF)
                load(w_in, p * (2 * P) + HQ)

            gla_head(GH - 1, lambda: hgrn_fq(0))

            def hgrn_pair(p, sub, after):
                load(w_in, p * (2 * P) + HI)
                wait(sp_, s0_out[sub], k.now(f"s0_out{sub}", 0, 16))
                for s in (2 * sub, 2 * sub + 1):
                    wait(sp_, s0_out[s], 16 * 2 * GH)
                for j in range(2):
                    sp_.dma_start(s0h[sub][:, :, j, :], sh[:, ds(p * 2 + j, 1)].rearrange("b o k v -> k (b o) v")).then_inc(s0_in[sub], 16)
                load(w_in, p * (2 * P) + HG)
                load(w_in, p * (2 * P) + MB)
                after()
                k.add("sample_ready", 2 * B)
                wait(sp_, S.sample_ready, k.now("sample_ready"))
                for j in range(2):
                    sp_.dma_start(out["hgrn_s"][0][:, ds(p * 2 + j, 1)].rearrange("b o k v -> k (b o) v"), s0h[sub][:, :, j, :]).then_inc(s0_out[sub], 16)
                k.add(f"s0_out{sub}", 2)
                k.add("state_ready", 2 * NC)
                wait(sp_, S.state_ready, k.now("state_ready"))
                sp_.dma_start(out["hgrn_p"][0, 0, ds(p * 2, 2)].rearrange("j k v -> k j v"), sp[0][:, :, 0:P]).then_inc(S.pstate_out, 16)

            with k.turns(sp_, "hgrn", HH // 4 - 1) as i:
                hgrn_pair(i * 2, 0, lambda: hgrn_fq(i * 2 + 1))
                hgrn_pair(i * 2 + 1, 1, lambda: hgrn_fq(i * 2 + 2))
            last = HH // 2 - 2
            hgrn_pair(last, 0, lambda: hgrn_fq(last + 1))

            def wout_first():
                load(a["w_out"][0], 0)
                load(a["w_out"][0], 2 * P)
            hgrn_pair(last + 1, 1, wout_first)
            wait(sp_, S.mixed, GH + HH // 2)
            for s in range(2):
                wait(sp_, s0_out[s], k.now(f"s0_out{s}", 0, 16))
            wait(sp_, S.pstate_out, 16 * (GH + HH // 2))
            sp_.dma_start(xres[:, 0:2, :], a["x_prompt"][0].rearrange("(b p) d -> p b d", p=P)).then_inc(S.x_in, 16)
            sp_.dma_start(xres[0:NS, 2, :], a["x_sample"].rearrange("b l d -> (b l) d")).then_inc(S.x_in, 16)
            with k.turns(sp_, "wout", 3) as i:
                for s in range(2):
                    load(a["w_out"][0], i * (4 * P) + (2 + s) * 2 * P)
            with k.turns(sp_, "memq", 4) as i:
                for s in range(2):
                    load(a["w_mem_q"][0], i * (4 * P) + s * 2 * P)
            for s in range(2):
                wait(sp_, mem_out[s], 8 * 16)
            wait(sp_, tile_done, 2 * (16 + 1 + 32 + 40 + 8))
            ck, cv_ = a["cache_mem_k"][0], a["cache_mem_v"][0]
            tiles_of = lambda ap: ap.rearrange("(t p) d -> p t d", p=P)
            for h in range(MH):
                sp_.dma_start(kc[:, h], tiles_of(out["mem_k"][0, 0][:, h])).then_inc(kc_in[h], 16)
                sp_.dma_start(vc[:, h], tiles_of(out["mem_v"][0, 0][:, h])).then_inc(vc_in[h], 16)

            load(a["w_mem_o"][0], 0)
            load(a["w_mem_o"][0], 2 * P)
            with k.turns(sp_, "xattn", B) as b:
                for h in range(MH):
                    k.add("k_turned", 2)
                    wait(sp_, S.k_turned, k.now("k_turned"))
                    sp_.dma_start(kc[:, h], ck[ds(b, 1), :, h].rearrange("o (t p) d -> p (o t) d", p=P)).then_inc(kc_in[h], 16)
                for h in range(MH):
                    wait(sp_, S.v_used, k.next("v_used"))
                    sp_.dma_start(vc[:, h], cv_[ds(b, 1), :, h].rearrange("o (t p) d -> p (o t) d", p=P)).then_inc(vc_in[h], 16)
            with k.turns(sp_, "memo", 3) as i:
                for s in range(2):
                    load(a["w_mem_o"][0], i * (4 * P) + (2 + s) * 2 * P)

            def load_up(j):
                s = begin_load()
                for half, col in ((0, 0), (1, FF)):
                    sp_.dma_start(raw[s][:, :, half * P:half * P + P], rows_of(w_up)[:, :, ds(j * P + col, P)]).then_inc(landed[s], 16)

            sc = a["state_ffn_conv"][0].rearrange("b j f -> (b j) f")
            wait(sp_, S.mo_split, B)
            sp_.dma_start(crow[0:16, :], sc[:, 0:CPART * P]).then_inc(S.conv_in, 16)
            sp_.dma_start(crow1[:], sc[:, CPART * P:FF]).then_inc(S.conv_in, 16)
            for g, (j0, nk) in enumerate(GROUPS):
                with k.turns(sp_, f"up{g}", nk // 2) as i:
                    for s in range(2):
                        load_up(i * 2 + (j0 + s))
                if nk % 2:
                    load_up(j0 + nk - 1)
                with k.turns(sp_, f"down{g}", 4) as i:
                    for s in range(2):
                        load(a["w_ffn_down"][0][j0 * P:(j0 + nk) * P], i * (4 * P) + s * 2 * P, nk)
            for part, (j0, n) in enumerate(((0, CPART), (CPART, FT - CPART))):
                wait(sp_, S.crow_copied, (j0 + n + 3) // 4)
                c = slice(j0 * P, (j0 + n) * P)
                sp_.dma_start(out["conv_p"][0, 0][:, c], crow[0:2, 0:n * P]).then_inc(S.conv_out, 16)
                sp_.dma_start(out["conv_s"][0].rearrange("b j f -> (b j) f")[:, c], crow[2:18, 0:n * P]).then_inc(S.conv_out, 16)
            n = 0
            for t4 in range(4):
                for blk in range(3):
                    n += 1
                    wait(sp_, S.y_copied, n)
                    cols = slice(t4 * 4 * P, (t4 + 1) * 4 * P)
                    if blk < 2:
                        sp_.dma_start(out["y_p"][0, blk * P:(blk + 1) * P, cols], ytok[:, blk, cols]).then_inc(S.y_out, 16)
                    else:
                        sp_.dma_start(out["y_s"].rearrange("b l d -> (b l) d")[:, cols], ytok[0:NS, 2, cols]).then_inc(S.y_out, 16)
            sp_.wait_ge(S.y_out, 16 * 12)
            sp_.wait_ge(S.conv_out, 64)
            sp_.wait_ge(S.pstate_out, 16 * (GH + HH // 2))
            for s in range(4):
                sp_.wait_ge(s0_out[s], k.now(f"s0_out{s}", 0, 16))
            for s in range(2):
                sp_.wait_ge(mem_out[s], 8 * 16)

        @block.gpsimd
        def _(pool):
            pool.memset(parrow[:], 0.0).then_inc(S.rows_cleared, 1)
            pool.memset(ident[:], 0.0).then_inc(S.made, 1)
            pool.memset(ones[:], 1.0).then_inc(S.made, 1)
            pool.memset(causal[:], 1.0).then_inc(S.made, 1)
            pool.memset(causal8[:], 1.0).then_inc(S.made, 1)
            pool.memset(own8[:], 1.0).then_inc(S.made, 1)
            pool.memset(keep[:], 1.0).then_inc(S.made, 1)
            pool.wait_ge(S.made, 6)
            pool.affine_select(out=ident[:], in_=ident[:], compare_op=ALU.not_equal, fill=1.0, base=0,
                               pattern=[[-1, P]], channel_multiplier=1).then_inc(S.made, 1)
            v = causal[:].rearrange("p (n c) -> p n c", c=C)
            pool.affine_select(out=v, in_=v, compare_op=ALU.is_ge, fill=0.0, base=0,
                               pattern=[[C, CPB], [1, C]], channel_multiplier=-1).then_inc(S.made, 1)
            v8 = causal8[:].rearrange("p (n c) -> p n c", c=L)
            pool.affine_select(out=v8, in_=v8, compare_op=ALU.is_ge, fill=0.0, base=0,
                               pattern=[[L, B], [1, L]], channel_multiplier=-1).then_inc(S.made, 1)
            pool.affine_select(out=own8[:], in_=own8[:], compare_op=ALU.is_ge, fill=0.0, base=0,
                               pattern=[[-L, B]], channel_multiplier=1).then_inc(S.made, 1)
            pool.memset(keep[:, 0:NP:C], 0.0).then_inc(S.made, 1)
            pool.memset(keep[:, NP:NT:L], 0.0).then_inc(S.made, 1)
            pool.wait_ge(S.made, 12)
            pool.affine_select(out=v, in_=v, compare_op=ALU.is_ge, fill=0.0, base=0,
                               pattern=[[-C, CPB], [0, C]], channel_multiplier=1).then_inc(S.made, 1)
            pool.affine_select(out=v8, in_=v8, compare_op=ALU.is_ge, fill=0.0, base=0,
                               pattern=[[-L, B], [0, L]], channel_multiplier=1).then_inc(S.made, 1)
            pool.affine_select(out=own8[:], in_=own8[:], compare_op=ALU.is_ge, fill=0.0, base=L - 1,
                               pattern=[[L, B]], channel_multiplier=-1).then_inc(S.made, 1)
            k = Counts("pool")
            with k.turns(pool, "split", NTILES // 4):
                for t in range(4):
                    wait(pool, high_ready, k.next("tile"))
                    half = raw[t // 2][:, :, (t % 2) * P:(t % 2) * P + P]
                    pool.tensor_tensor(wL[t % 2][:], half, wH[t % 2][:].bitcast(F32), ALU.subtract).then_inc(low_ready, 1)
            for t in range(NTILES % 4):
                wait(pool, high_ready, k.next("tile"))
                half = raw[t // 2][:, :, (t % 2) * P:(t % 2) * P + P]
                pool.tensor_tensor(wL[t % 2][:], half, wH[t % 2][:].bitcast(F32), ALU.subtract).then_inc(low_ready, 1)

        @block.tensor
        def _(pe):
            k = Counts("pe")

            def begin_tile():
                s = k.slot("tile", 2)
                wait(pe, bank_free[s], k.rounds("tile", 2))
                k.add("tile")
                wait(pe, high_ready, k.now("tile"))
                return s

            def tile(nk=KT, mov=(hH, hL), ready=None, extra=None, done=1, cols=NT, work=()):
                s = begin_tile()
                dst = PB[s][:, 0:cols]
                work = sorted(work, key=lambda w: w[0])

                def between(place):
                    while work and work[0][0] <= place:
                        work.pop(0)[1]()

                for t in range(nk):
                    between(2 * t)
                    if ready and t % 4 == 0:
                        wait(pe, ready[0], ready[1] + t // 4)
                    pe.matmul(dst, wH[s][:, t, :], mov[0][:, t, :], start=(t == 0), stop=False)
                    pe.matmul(dst, wH[s][:, t, :], mov[1][:, t, :], start=False, stop=False)
                wait(pe, low_ready, k.now("tile", 1 - done))
                if extra:
                    extra(s)
                for t in range(nk):
                    between(2 * nk + t)
                    mm = pe.matmul(dst, wL[s][:, t, :], mov[0][:, t, :], start=False, stop=(t == nk - 1))
                if done == 2:
                    k.add("tile")
                mm.then_inc(tile_done, done)

            def memory_turn(t):
                wait(pe, bank_free[t % 2], k.rounds("memturn", 2, more=1))
                wait(pe, S.mem_copied, k.now("memturn", min(t, 1)))
                for b in range(2):
                    mm = pe.transpose(T[t % 2][:, b * P:(b + 1) * P], memf[t % 2][:, b * P:(b + 1) * P], ident[:])
                mm.then_inc(S.mem_turned, 1)
                k.add("memturn")

            def memory_tiles(name):
                def four(first):
                    for t in range(4):
                        turn = [(24, lambda t=t: memory_turn((t - 1) % 4))] if t or not first else []
                        tile(mov=(mH, mL), cols=M, work=turn)
                four(True)
                with k.turns(pe, name, 3):
                    four(False)

            pe.wait_ge(S.made, 15)
            pe.wait_ge(S.par_in, 16 * len(PAR))
            for blk in range(PBLK):
                mm = pe.transpose(T[0][:, blk * P:(blk + 1) * P], parrow[:, blk, :], ident[:])
            mm.then_inc(S.par_turned, 1)
            pe.wait_ge(S.tok_scaled, 2)
            rnd = 0
            for r in range(KT // 2):
                if rnd >= 4:
                    pe.wait_ge(S.tok_low, rnd - 3)
                for t in range(2):
                    for b in range(2):
                        mm = pe.transpose(RB[rnd % 4][:, t * M + b * P:t * M + (b + 1) * P], mtok[:, b, (2 * r + t) * P:(2 * r + t + 1) * P], ident[:])
                mm.then_inc(S.tok_turned, 1)
                rnd += 1
            pe.wait_ge(S.tok_low, rnd)
            memory_tiles("mem_k")
            pe.wait_ge(S.tok_scaled, 5)
            for t in range(KT):
                pe.wait_ge(S.tok_low, rnd - 3)
                for b in range(3):
                    n = P if b < 2 else NS
                    mm = pe.transpose(RB[rnd % 4][:, b * P:b * P + n], xtok[0:n, b, t * P:(t + 1) * P], ident[0:n, 0:n])
                mm.then_inc(S.tok_turned, 1)
                rnd += 1
            memory_turn(3)
            memory_tiles("mem_v")
            pe.wait_ge(S.tok_low, rnd)
            tile(done=2, work=[(24, lambda: memory_turn(3))])
            pe.wait_ge(S.mem_copied, 2 * KT)

            def turn_round(srcs, first=False):
                r = k.slot("turned", 2)
                wait(pe, S.turn_copied, k.now("turned", 0 if first else 1))
                for b in range(3):
                    n = P if b < 2 else NS
                    mm = pe.transpose(T[r][0:n, b * P:(b + 1) * P], srcs[:, b * P:b * P + n], ident[:])
                mm.then_inc(S.turned, 1)
                k.add("turned")

            def tile_copied(back):
                s = (k.n["tile"] - 1 - back) % 2
                wait(pe, bank_free[s], k.rounds("tile", 2, 1 + back, more=1))

            def scores(heads, nk):
                for j in range(heads):
                    for c0, n in ((0, P), (P, P), (NP, NS)):
                        for t in range(nk):
                            u = j if heads == 2 else t
                            mm = pe.matmul(KV[j][0:n, c0:c0 + n], ki[:, u, c0:c0 + n], qd[:, u, c0:c0 + n], start=(t == 0), stop=(t == nk - 1))
                mm.then_inc(S.scores_done, 1)

            def kv_mm(u, rows, blk, keys, wide, kind, first):
                other = {"state_ready": "sample_ready", "sample_ready": "state_ready"}[kind]
                if first:
                    wait(pe, getsem[other], k.now(other))
                else:
                    wait(pe, getsem[kind], k.now(kind, 1))
                col = 0 if wide == GV else u * P
                pe.matmul(KV[u][:, 0:wide], keys, vtok[rows, blk, col:col + wide], start=True, stop=True).then_inc(S.kv_done, 1)
                k.add(kind)

            getsem = {"state_ready": S.state_ready, "sample_ready": S.sample_ready}

            def inter(n, heads, blk):
                for j in range(heads):
                    nv, nk = (1, 1) if heads == 2 else (4, 2)
                    for v in range(nv):
                        for t in range(nk):
                            u = j if heads == 2 else t
                            dst = O[j][:, n * C:(n + 1) * C] if heads == 2 else O[blk][:, v * P + n % CPB * C:v * P + n % CPB * C + C]
                            last = n % CPB == CPB - 1 and v == nv - 1 and t == nk - 1
                            mm = pe.matmul(dst, sp[n % 2][:, u, v * P:(v + 1) * P], qi[:, u, n * C:(n + 1) * C],
                                           start=False, stop=last and heads == 1, skip_group_check=True)
                mm.then_inc(S.inter_done, 1)

            def chunk(n, heads, place, gap):
                blk, i = n // CPB, n % CPB
                rows = slice(i * C, (i + 1) * C)

                def product():
                    for u in range(2):
                        kv_mm(u, rows, blk, ktok[rows, blk, u * P:(u + 1) * P], GV if heads == 1 else P, "state_ready", n == 0)

                def queries():
                    wait(pe, S.state_ready, k.now("state_ready", 2))
                    inter(n, heads, blk)
                return [(place, product)] + ([(place + gap, queries)] if n else [])

            def sample(bs, heads):
                for b in bs:
                    s = b % 4 if heads == 1 else k.slot("pair", 2)
                    c0 = NP + b * L
                    for j in range(heads):
                        nv, nk = (1, 1) if heads == 2 else (4, 2)
                        for v in range(nv):
                            for t in range(nk):
                                u = j if heads == 2 else t
                                st = s0h[s][:, b, u, :] if heads == 2 else s0g[s][:, t, v * P:(v + 1) * P]
                                dst = O[j][:, c0:c0 + L] if heads == 2 else O[0][:, v * NS + b * L:v * NS + (b + 1) * L]
                                mm = pe.matmul(dst, st, qd[:, u, c0:c0 + L], start=False, stop=(b == B - 1), skip_group_check=True)
                    if b == B - 1:
                        mm.then_inc(S.o_done, 1)
                    for u in range(2):
                        kv_mm(u, slice(0, NS), 2, kmask[:, b, u * P:(u + 1) * P], GV if heads == 1 else P, "sample_ready", b == 0)

            def intra_gla(blk):
                for v in range(4):
                    pe.matmul(O[blk][:, v * P:(v + 1) * P], vtok[:, blk, v * P:(v + 1) * P], bd[:, 0, blk * P:(blk + 1) * P],
                              start=(v == 0), stop=False, skip_group_check=True)

            tile_copied(0)
            tile_copied(1)
            def decay_logits():
                wait(pe, S.wa_in, k.next("wa", 16))
                wait(pe, S.turn_copied, k.now("turned"))
                wait(pe, S.alog_used, k.now("prep", 0, 2))
                for j in range(2):
                    pe.matmul(T[j][:, 0:NT], wah[:, j * P:(j + 1) * P], gaT[:], start=True, stop=True).then_inc(S.alog_done, 1)

            def turn_keys_first():
                wait(pe, S.prep_ready, k.now("prep"))
                turn_round(ke[:, 0], True)

            def turn_last(v):
                tile_copied(1)
                turn_round(vo[:, v])

            def score_work(heads):
                wait(pe, S.sample_ready, k.now("sample_ready"))
                scores(heads, 3 - heads)

            def outputs_free():
                wait(pe, S.turn_copied, k.now("turned"))
                wait(pe, S.scores_kept, k.now("prep"))
                wait(pe, S.o_copied, k.now("o"))
                wait(pe, S.ss_used, k.now("ss"))

            def gla_first():
                outputs_free()
                intra_gla(0)

            def gla_samples_first():
                k.add("o", 2)
                wait(pe, S.kmask_ready, k.now("prep"))
                wait(pe, S.o_copied, k.now("o", 1))
                for v in range(4):
                    pe.matmul(O[0][:, v * NS:(v + 1) * NS], vtok[0:NS, 2, v * P:(v + 1) * P], bds[:, 0, :],
                              start=(v == 0), stop=False, skip_group_check=True)

            def gla_sample(b):
                wait(pe, s0_in[b % 4], k.next(f"s0_in{b % 4}", 16))
                sample([b], 1)
                if b == B - 1:
                    k.add("o")

            def gla_norm():
                wait(pe, S.squares_ready, k.now("prep"))
                for v in range(4):
                    mm = pe.matmul(O[1][:, 0:NT], ones[:], sqg[:, v, :], start=(v == 0), stop=(v == 3))
                mm.then_inc(S.ss_done, 1)
                k.add("ss")

            with k.turns(pe, "gla", GH) as h:
                tile()
                tile()
                tile(work=[(4, decay_logits)])
                for t in range(3):
                    tile()
                k.add("prep")
                tile(work=[(8, turn_keys_first), (22, lambda: turn_round(ke[:, 1]))])
                tile(work=[(4, lambda: turn_round(vo[:, 0])), (18, lambda: turn_round(vo[:, 1])), (34, lambda: turn_last(2))])
                tile(work=[(12, lambda: turn_last(3)), (26, lambda: score_work(1))])
                tile(work=[(4, gla_first)] + chunk(0, 1, 6, 6) + chunk(1, 1, 18, 6) + chunk(2, 1, 32, 6))
                tile(work=chunk(3, 1, 2, 6) + [(16, lambda: intra_gla(1))] + chunk(4, 1, 18, 6) + chunk(5, 1, 32, 6))
                tile(work=chunk(6, 1, 2, 6) + chunk(7, 1, 16, 6) + [(30, gla_samples_first), (34, lambda: gla_sample(0))])
                tile(work=[(4, lambda: gla_sample(1)), (18, lambda: gla_sample(2)), (32, lambda: gla_sample(3))])
                tile()
                tile(work=[(10, lambda: gla_sample(4)), (32, lambda: gla_sample(5))])
                tile(work=[(2, lambda: gla_sample(6)), (16, lambda: gla_sample(7)), (42, gla_norm)])

            def pair_first():
                outputs_free()
                for j in range(2):
                    for blk in range(2):
                        pe.matmul(O[j][:, blk * P:(blk + 1) * P], vtok[:, blk, j * P:(j + 1) * P], bd[:, j, blk * P:(blk + 1) * P],
                                  start=(blk == 0), stop=False, skip_group_check=True)
                    pe.matmul(O[j][:, NP:NT], vtok[0:NS, 2, j * P:(j + 1) * P], bds[:, j, :], start=False, stop=False, skip_group_check=True)

            def pair_samples_first():
                wait(pe, S.kmask_ready, k.now("prep"))
                sub = k.slot("pair", 2)
                k.add(f"s0_in{sub}", 2)
                wait(pe, s0_in[sub], k.now(f"s0_in{sub}", 0, 16))

            def pair_norm():
                wait(pe, S.squares_ready, k.now("prep"))
                for j in range(2):
                    mm = pe.matmul(O[j][:, 0:NT], ones[:], sqg[:, j, :], start=True, stop=True)
                mm.then_inc(S.ss_done, 1)
                k.add("ss")

            def hgrn_pair():
                for t in range(6):
                    tile()
                k.add("prep")
                tile(work=[(6, turn_keys_first), (14, lambda: turn_round(ke[:, 1])), (22, lambda: score_work(2)),
                           (32, lambda: turn_round(vo[:, 0])), (40, lambda: turn_last(1))])
                tile(work=[(5, pair_first)] + [w for n in range(NC) for w in chunk(n, 2, 6 + 5 * n, 3)])
                tile(work=[(3, pair_samples_first)] + [(4 + 5 * b, lambda b=b: sample([b], 2)) for b in range(B)])
                k.add("o", 2)
                k.add("pair")
                tile(work=[(30, pair_norm)])

            with k.turns(pe, "hgrn", HH // 4):
                hgrn_pair()
                hgrn_pair()

            def residual(s):
                x_slot = k.slot("xst", 2)
                wait(pe, S.xst_ready, k.next("xst"))
                for b in range(3):
                    n = P if b < 2 else NS
                    pe.matmul(PB[s][:, b * P:b * P + n], xst[x_slot][0:n, b, :], ident[0:n, 0:n],
                              start=False, stop=False, skip_group_check=True)

            with k.turns(pe, "wout", 4):
                for t in range(4):
                    tile(ready=(S.mix_split, 1), extra=residual)

            def sum_squares(n):
                pe.wait_ge(S.acc_ready, n)
                pe.matmul(T[0][:, 0:NT], ones[:], acc[:], start=True, stop=True).then_inc(S.sum_done, 1)
            sum_squares(1)
            with k.turns(pe, "memq", 4):
                for t in range(4):
                    tile(ready=(S.normed, 1))

            def turn_keys(h):
                wait(pe, kc_in[h], k.next(f"kc{h}", 16))
                for r in range(2):
                    s = k.slot("kturn", 4)
                    cp = (S.kT_even, S.kT_odd)[s % 2]
                    wait(pe, cp, k.rounds("kturn", 2, 2))
                    for dt in range(2):
                        for mt in range(2):
                            mm = pe.transpose(RB[s][:, dt * M + mt * P:dt * M + (mt + 1) * P],
                                              kc[:, h, mt, (2 * r + dt) * P:(2 * r + dt + 1) * P], ident[:])
                    mm.then_inc(S.k_turned, 1)
                    k.add("kturn")

            def keys_copied():
                wait(pe, S.kT_even, k.rounds("kturn", 2))
                wait(pe, S.kT_odd, k.rounds("kturn", 2))

            pe.wait_ge(bank_free[0], k.now("tile") // 2)
            pe.wait_ge(bank_free[1], k.now("tile") // 2)
            for h in range(MH):
                turn_keys(h)
                keys_copied()
                if h:
                    pe.wait_ge(S.pp_ready, h)
                for lt in range(2):
                    for dt in range(4):
                        mm = pe.matmul(T[0][:, lt * M:(lt + 1) * M], q[:, 4 * h + dt, lt * P:(lt + 1) * P], kT[:, h, dt, :],
                                       start=(dt == 0), stop=(dt == 3))
                mm.then_inc(S.sp_done, 1)
                pe.wait_ge(S.pp_ready, h + 1)
                if h:
                    pe.wait_ge(S.ppT_copied, h)
                for lt in range(2):
                    for mt in range(2):
                        mm = pe.transpose(T[1][:, mt * NP + lt * P:mt * NP + (lt + 1) * P], pP[:, lt, mt * P:(mt + 1) * P], ident[:])
                mm.then_inc(S.ppT_done, 1)
                pe.wait_ge(S.ppT_copied, h + 1)
                wait(pe, vc_in[h], k.next(f"vc{h}", 16))
                for dt in range(4):
                    n = 4 * h + dt
                    if n >= 2:
                        pe.wait_ge(S.mop_split, n - 1)
                    for mt in range(2):
                        mm = pe.matmul(PB[n % 2][:, 0:NP], vc[:, h, mt, dt * P:(dt + 1) * P], pTP[:, mt, :], start=(mt == 0), stop=(mt == 1))
                    mm.then_inc(S.mop_done if dt < 3 else S.v_used, 1)
            pe.wait_ge(S.mop_split, 16)
            with k.turns(pe, "xattn", B) as b:
                for h in range(MH):
                    turn_keys(h)
                    if h == MH - 1:
                        keys_copied()
                wait(pe, S.pT_copied, k.now("smp"))
                for h in range(MH):
                    for mt in range(2):
                        for dt in range(4):
                            mm = pe.matmul(T[0][:, mt * 32 + h * L:mt * 32 + (h + 1) * L], kT[:, h, dt, mt * P:(mt + 1) * P],
                                           q[:, 4 * h + dt, ds(b * L + NP, L)], start=(dt == 0), stop=(dt == 3))
                mm.then_inc(S.sT_done, 1)
                k.add("smp")
                wait(pe, S.sT_copied, k.now("smp"))
                for mt in range(2):
                    mm = pe.transpose(T[1][0:32, mt * P:(mt + 1) * P], sTs[:, mt * 32:(mt + 1) * 32], ident[:])
                mm.then_inc(S.s_done, 1)
                wait(pe, S.p_ready, k.now("smp"))
                for mt in range(2):
                    mm = pe.matmul(T[0][:, 64 + mt * 32:64 + (mt + 1) * 32], pr[:, mt * P:(mt + 1) * P], ident[0:32, 0:32],
                                   start=True, stop=True)
                mm.then_inc(S.pT_done, 1)
                wait(pe, S.pT_copied, k.now("smp"))
                wait(pe, S.mo_split, k.now("smp", 1))
                for h in range(MH):
                    wait(pe, vc_in[h], k.next(f"vc{h}", 16))
                    for dt in range(4):
                        for mt in range(2):
                            mm = pe.matmul(PB[0][:, (4 * h + dt) * L:(4 * h + dt + 1) * L], vc[:, h, mt, dt * P:(dt + 1) * P],
                                           pTs[:, mt, h * L:(h + 1) * L], start=(mt == 0), stop=(mt == 1))
                    mm.then_inc(S.v_used, 1)
            wait(pe, S.mo_split, B)
            with k.turns(pe, "memo", 4):
                for t in range(4):
                    tile()
            sum_squares(2)

            pe.wait_ge(S.conv_in, 32)
            for part, rows, n in ((0, crow, CPART), (1, crow1, FT - CPART)):
                pe.wait_ge(S.normed, 8) if part == 0 else pe.wait_ge(S.conv_cols, 1)
                for j in range(n):
                    mm = pe.transpose(T[1][:, j * 16:(j + 1) * 16], rows[0:16, j * P:(j + 1) * P], ident[0:16, 0:16])
                mm.then_inc(S.conv_turned, 1)
            def up():
                for t in range(2):
                    tile(ready=(S.normed, 5))

            def history_rows():
                pe.wait_ge(S.ug_kept, FT)
                for n, j0 in enumerate(range(0, FT, 4)):
                    if n >= 2:
                        pe.wait_ge(S.crow_copied, n - 1)
                    for j in range(min(4, FT - j0)):
                        mm = pe.transpose(RB[n % 2][0:18, j * P:(j + 1) * P], cnew[:, j0 + j, :], ident[:])
                    mm.then_inc(S.crow_turned, 1)

            for g, (j0, nk) in enumerate(GROUPS):
                with k.turns(pe, f"up{g}", nk // 2):
                    up()
                    up()
                if nk % 2:
                    up()
                with k.turns(pe, f"down{g}", 4):
                    for t in range(4):
                        tile(nk, (aH, aL), ready=(S.act4, 4 * g + 1))
            history_rows()
            sum_squares(3)
            n = 0
            for t4 in range(4):
                pe.wait_ge(S.y_normed, t4 + 1)
                for b in range(3):
                    w = P if b < 2 else NS
                    bank = (KV[0], KV[1])[n % 2]
                    if n >= 2:
                        pe.wait_ge(S.y_copied, n - 1)
                    for t in range(4):
                        mm = pe.transpose(bank[0:w, t * P:(t + 1) * P], x[:, 4 * t4 + t, b * P:b * P + w], ident[:])
                    mm.then_inc(S.y_turned, 1)
                    n += 1

        @block.scalar
        def _(act):
            k = Counts("act")

            def own(ins):
                ins.then_inc(S.act_step, 1)
                k.add("step")

            def settle():
                wait(act, S.act_step, k.now("step"))

            def ahead():
                s = k.slot("ahead", 4)
                wait(act, landed[s // 2], k.rounds("ahead", 4, 0, 32, more=1))
                half = raw[s // 2][:, :, (s % 2) * P:(s % 2) * P + P]
                act.activation(wH[s % 2][:], half, ACT.Copy).then_inc(high_ready, 1)
                k.add("ahead")

            def step(more=True):
                s = k.slot("tile", 2)
                wait(act, tile_done, k.next("tile"))
                if more:
                    ahead()
                return s

            def evac(dst, scale=1.0, more=True):
                s = step(more)
                act.activation(dst, PB[s][:, 0:NT], ACT.Copy, scale=scale).then_inc(bank_free[s], 1)

            def root_guess(v, g):
                wait(act, S.mean_ready, k.next("root"))
                own(act.activation(g, v, ACT.Ln))
                settle()
                act.activation(g, g, ACT.Exp, scale=-0.5).then_inc(S.root_ready, 1)

            def squares(b, n):
                wait(act, S.tok_squared, k.now("squared"))
                k.add("squared")
                act.activation(sqtok[0:n, :], (mtok[:, b, :] if b < 2 else xtok[0:n, b - 2, :]), ACT.Square,
                               accum_out=small[0:n, b:b + 1]).then_inc(S.tok_squared, 1)

            act.wait_ge(S.mem_in, 16)
            act.wait_ge(S.small_cleared, 1)
            squares(0, P)
            squares(1, P)
            root_guess(small[:, 5:7], small[:, 10:12])
            act.wait_ge(S.par_turned, 1)
            act.activation(par[:], T[0][:, 0:PBLK * P].rearrange("p (b n) -> p b n", n=P), ACT.Copy).then_inc(S.par_ready, 1)
            act.wait_ge(S.par_ready, 1)
            for r in range(KT // 2):
                act.wait_ge(S.tok_turned, r + 1)
                for t in range(2):
                    ins = act.activation(mH[:, 2 * r + t, :], RB[r % 4][:, t * M:(t + 1) * M], ACT.Identity, scale=pcol("mem", 2 * r + t))
                ins.then_inc(S.tok_high, 1)
            ahead()
            ahead()
            act.wait_ge(S.lb_shifted, 1)
            act.activation(small[:, 32:64], small[:, 32:64], ACT.Exp).then_inc(S.lb_exp, 1)

            def rows_of_memory(dst):
                def rows(col, t):
                    m = t // 2
                    wait(act, S.mem_turned, k.next("memturn"))
                    if t % 2 == 0:
                        wait(act, mem_out[m], k.now(f"memo{m}", 0, 16))
                    act.activation(memo[m][:, :, (t % 2) * P:(t % 2 + 1) * P], T[t % 2][:, 0:M].rearrange("p (b n) -> p b n", b=2),
                                   ACT.Copy).then_inc(S.mem_copied, 1)
                    if t % 2:
                        wait(act, S.mem_copied, k.now("memturn"))
                        act.dma_start(dst[:, :, ds(col, 2 * P)], memo[m][:]).then_inc(mem_out[m], 16)
                        k.add(f"memo{m}")

                def four(col, first=False):
                    for t in range(4):
                        s = step()
                        act.activation(memf[s][:], PB[s][:, 0:M], ACT.Copy).then_inc(bank_free[s], 1)
                        if t:
                            rows(col + (t - 1) // 2 * 2 * P, t - 1)
                        elif not first:
                            rows(col - 2 * P, 3)
                return rows, four

            rows, four = rows_of_memory(mk_out)
            four(0, True)
            four(4 * P)
            act.wait_ge(S.x_in, 32)
            for b in range(2, 5):
                squares(b, P if b < 4 else NS)
            root_guess(small[:, 7:10], small[:, 12:15])
            with k.turns(act, "mem_k1", 2) as i:
                four(i * (4 * P) + 8 * P)
            for t in range(KT):
                act.wait_ge(S.tok_turned, KT // 2 + t + 1)
                act.activation(hH[:, t, :], RB[t % 4][:, 0:NT], ACT.Identity, scale=pcol("mix", t)).then_inc(S.tok_high, 1)
            rows(D - 2 * P, 3)
            rows, four = rows_of_memory(mv_out)
            four(0, True)
            with k.turns(act, "mem_v", 3) as i:
                four(i * (4 * P) + 4 * P)
            rows(D - 2 * P, 3)

            s = step()
            step()
            for half in range(2):
                c = slice(half * NT // 2, (half + 1) * NT // 2)
                act.activation(gaT[:, c], PB[s][0:16, c], ACT.Copy).then_inc(bank_free[(s + half) % 2], 1)

            def copy_round(dst, j, nv=1):
                r = k.slot("turned", 2)
                wait(act, S.turned, k.next("turned"))
                c = slice(j * P, (j + 1) * P)
                act.activation(dst[:, 0:2, c], T[r][:, 0:2 * P].rearrange("p (b n) -> p b n", b=2), ACT.Copy)
                act.activation(dst[0:NS, 2, c], T[r][0:NS, 2 * P:3 * P], ACT.Copy).then_inc(S.turn_copied, 1)

            def gate_exp():
                s = step()
                act.activation(ge[s][:], PB[s][:, 0:NT], ACT.Exp, scale=-1.0).then_inc(S.gate_exp, 1)

            def exps():
                wait(act, S.decay_ready, k.next("decay"))
                act.activation(e1[:], cmid[:], ACT.Exp)
                act.activation(e2[:], cmid[:], ACT.Exp, scale=-1.0)
                act.activation(emid[:], cum[:, :, C // 2 - 1:NP:C], ACT.Exp)
                act.activation(elast[:], cum[:, :, C - 1:NP:C], ACT.Exp).then_inc(S.exps_ready, 1)

            with k.turns(act, "gla", GH) as h:
                evac(qd[:, 0, :], GK ** -0.5)
                evac(qd[:, 1, :], GK ** -0.5)
                wait(act, S.mixed, k.now("mix"))
                for j in range(2):
                    wait(act, S.alog_done, k.next("alog"))
                    act.activation(e1[:, j, :], T[j][:, 0:NT], ACT.Abs, bias=pcol("ba", h * 2 + j)).then_inc(S.abs_ready, 1)
                wait(act, S.abs_ready, k.now("alog"))
                own(act.activation(e1[:], e1[:], ACT.Exp, scale=-1.0))
                settle()
                act.activation(e1[:], e1[:], ACT.Ln, bias=ones[:, 0:1]).then_inc(S.ln_ready, 1)
                evac(ki[:, 0, :])
                exps()
                evac(ki[:, 1, :])
                evac(vo[:, 0, :])
                evac(vo[:, 1, :])
                copy_round(ktok, 0)
                copy_round(ktok, 1)
                evac(vo[:, 2, :])
                copy_round(vtok, 0)
                copy_round(vtok, 1)
                copy_round(vtok, 2)
                evac(vo[:, 3, :])
                copy_round(vtok, 3)
                gate_exp()
                gate_exp()
                k.add("inter", CPB - 1)
                wait(act, S.inter_done, k.now("inter"))
                act.activation(vo[:, :, 0:P], O[0][:].rearrange("p (v n) -> p v n", v=4), ACT.Copy).then_inc(S.o_copied, 1)
                gate_exp()
                k.add("inter", CPB)
                wait(act, S.inter_done, k.now("inter"))
                act.activation(vo[:, :, P:NP], O[1][:].rearrange("p (v n) -> p v n", v=4), ACT.Copy).then_inc(S.o_copied, 1)
                for t in range(4):
                    gate_exp()
                wait(act, S.o_done, k.next("o"))
                act.activation(vo[:, :, NP:NT], O[0][:, 0:4 * NS].rearrange("p (v n) -> p v n", v=4), ACT.Copy).then_inc(S.o_copied, 1)
                wait(act, S.o_copied, k.now("o", 0, 3))
                act.activation(sqg[:], vo[:], ACT.Square).then_inc(S.squares_ready, 1)
                gate_exp()
                root_guess(rsg[:, 0, :], sqg[:, 0, :])
                k.add("mix")

            n_gla = 3 * GH

            def hgrn_pair():
                for j in range(2):
                    s = step()
                    if j == 0:
                        wait(act, S.mixed, k.now("mix"))
                    act.activation(e1[:, j, :], PB[s][:, 0:NT], ACT.Exp, scale=-1.0).then_inc(S.f_exp, 1)
                s = step()
                act.activation(e2[:, 0, :], PB[s][:, 0:NT], ACT.Exp, scale=-1.0).then_inc(S.gate_exp, 1)
                wait(act, S.f_ready, k.next("f"))
                act.activation(e1[:], cum[:], ACT.Ln).then_inc(S.ln_ready, 1)
                s = step()
                act.activation(e2[:, 1, :], PB[s][:, 0:NT], ACT.Exp, scale=-1.0).then_inc(S.gate_exp, 1)
                evac(vo[:, 0, :])
                exps()
                evac(vo[:, 1, :])
                copy_round(ktok, 0)
                copy_round(ktok, 1)
                copy_round(vtok, 0)
                copy_round(vtok, 1)
                gate_exp()
                gate_exp()
                wait(act, S.o_done, k.next("o"))
                for j in range(2):
                    act.activation(vo[:, j, :], O[j][:, 0:NT], ACT.Copy).then_inc(S.o_copied, 1)
                    k.add("o_copied")
                wait(act, S.o_copied, k.now("o_copied", -n_gla))
                act.activation(sqg[:, 0:2, :], vo[:, 0:2, :], ACT.Square).then_inc(S.squares_ready, 1)
                gate_exp()
                gate_exp()
                root_guess(rsg[:], sqg[:, 0:2, :])
                k.add("mix")

            with k.turns(act, "hgrn", HH // 4):
                hgrn_pair()
                hgrn_pair()

            act.wait_ge(S.mixed, GH + HH // 2)
            for g in range(4):
                act.activation(hH[:, 4 * g:4 * g + 4, :], omix[:, 4 * g:4 * g + 4, :], ACT.Copy).then_inc(S.mix_high, 1)

            def square_tile(i, t):
                s = step()
                wait(act, bank_free[s], k.rounds("tile", 2, 1, more=1))
                act.activation(sq[s][:], x[:, ds(i * 4 + t, 1), :].rearrange("p a n -> p (a n)"), ACT.Square).then_inc(S.sq_ready, 1)

            def norm_high():
                root_guess(rs[:], sq[0][:])
                for g in range(4):
                    wait(act, S.norm_tmp, k.next("norm"))
                    act.activation(hH[:, 4 * g:4 * g + 4, :], nrm[g % 2][:], ACT.Copy).then_inc(S.norm_high, 1)

            with k.turns(act, "wout", 4) as i:
                for t in range(4):
                    square_tile(i, t)
            norm_high()
            with k.turns(act, "memq", 4) as i:
                for t in range(4):
                    evac(q[:, ds(i * 4 + t, 1), :].rearrange("p a n -> p (a n)"), MD ** -0.5)

            def copy_keys(h):
                s = k.slot("kturn", 4)
                wait(act, S.k_turned, k.now("kturn", -1))
                act.activation(kT[:, h, 0:2, :], RB[s][:].rearrange("p (t n) -> p t n", t=2), ACT.Copy).then_inc(S.kT_even, 1)
                k.add("kturn", 2)

            for h in range(MH):
                copy_keys(h)
                act.wait_ge(S.pmax_ready, h + 1)
                for lt in range(2):
                    ins = act.activation(pP[:, lt, :], T[0][:, lt * M:(lt + 1) * M], ACT.Exp, bias=small[:, 2 + lt:3 + lt],
                                         accum_out=small[:, 4 + lt:5 + lt])
                ins.then_inc(S.pp_exp, 1)
                act.wait_ge(S.ppT_done, h + 1)
                act.activation(pTP[:], T[1][:].rearrange("p (m n) -> p m n", m=2), ACT.Copy).then_inc(S.ppT_copied, 1)
                for dt in range(4):
                    act.wait_ge(*((S.mop_done, 3 * h + dt + 1) if dt < 3 else (S.v_used, h + 1)))
                    act.activation(hH[:, 4 * h + dt, 0:NP], PB[dt % 2][:, 0:NP], ACT.Copy).then_inc(S.mop_high, 1)
            k.add("v_used", MH)
            with k.turns(act, "xattn", B) as b:
                for h in range(MH):
                    copy_keys(h)
                wait(act, S.sT_done, k.next("smp"))
                act.activation(sTs[:], T[0][:, 0:64], ACT.Copy).then_inc(S.sT_copied, 1)
                wait(act, S.max_ready, k.now("smp"))
                act.activation(pr[:], T[1][0:32, 0:M], ACT.Exp, bias=small[0:32, 9:10], accum_out=small[0:32, 10:11]).then_inc(S.p_exp, 1)
                wait(act, S.pT_done, k.now("smp"))
                act.activation(pTs[:], T[0][:, 64:128].rearrange("p (m n) -> p m n", m=2), ACT.Copy).then_inc(S.pT_copied, 1)
                k.add("v_used", MH)
                wait(act, S.v_used, k.now("v_used"))
                act.activation(hH[:, :, ds(b * L + NP, L)], PB[0][:, 0:P].rearrange("p (t n) -> p t n", t=KT), ACT.Copy).then_inc(S.mo_high, 1)
            with k.turns(act, "memo", 4) as i:
                for t in range(4):
                    square_tile(i, t)
            norm_high()

            for part, (j0, n) in enumerate(((0, CPART), (CPART, FT - CPART))):
                act.wait_ge(S.conv_turned, part + 1)
                act.activation(cin[:, j0:j0 + n, :], T[1][:, 0:16 * n].rearrange("p (j n) -> p j n", n=16), ACT.Copy).then_inc(S.conv_cols, 1)
            act.wait_ge(S.conv_cols, 2)

            def up(j, col, js):
                s = step()
                act.activation(seq[js][:, 2:2 + NP], PB[s][:, 0:NP], ACT.Copy)
                smp = seq[js][:, 2 + NP:NSEQ].rearrange("p (b n) -> p b n", b=B)
                act.activation(smp[:, :, 2:2 + L], PB[s][:, NP:NT].rearrange("p (b n) -> p b n", b=B), ACT.Copy).then_inc(bank_free[s], 1)
                act.activation(smp[:, :, 0:2], cin[:, ds(j, 1), :].rearrange("p a (b n) -> p (a b) n", b=B), ACT.Copy).then_inc(S.seq_ready, 1)
                step()
                wait(act, S.conv_ready, k.next("conv"))
                act.activation(ce[js][:, 0:NCONV], cv[js][:, 0:NCONV], ACT.Exp, scale=-1.0).then_inc(S.ce_ready, 1)
                wait(act, S.av_ready, k.now("conv"))
                act.activation(aH[:, ds(col, 1), :].rearrange("p a n -> p (a n)"), av[js][:], ACT.Copy).then_inc(S.act_high, 1)

            for g, (j0, nk) in enumerate(GROUPS):
                with k.turns(act, f"up{g}", nk // 2) as i:
                    up(i * 2 + j0, i * 2, 0)
                    up(i * 2 + (j0 + 1), i * 2 + 1, 1)
                if nk % 2:
                    up(j0 + nk - 1, nk - 1, 0)
                if g < 2:
                    with k.turns(act, f"down{g}", 4):
                        for t in range(4):
                            step()
                else:
                    with k.turns(act, "down2", 3) as i:
                        for t in range(4):
                            square_tile(i, t)
                    for t in range(4):
                        s = step(more=t < 2)
                        wait(act, bank_free[s], k.rounds("tile", 2, 1, more=1))
                        act.activation(sq[s][:], x[:, 12 + t, :], ACT.Square).then_inc(S.sq_ready, 1)
            for n, j0 in enumerate(range(0, FT, 4)):
                w = min(4, FT - j0)
                act.wait_ge(S.crow_turned, n + 1)
                if j0 == CPART:
                    act.wait_ge(S.conv_out, 32)
                c = (j0 % CPART) * P
                act.activation(crow[0:18, c:c + w * P], RB[n % 2][0:18, 0:w * P], ACT.Copy).then_inc(S.crow_copied, 1)
            root_guess(rs[:], sq[0][:])
            act.wait_ge(S.conv_out, 64)
            n = 0
            for t4 in range(4):
                for b in range(3):
                    w = P if b < 2 else NS
                    n += 1
                    act.wait_ge(S.y_turned, n)
                    act.activation(ytok[0:w, b, t4 * 4 * P:(t4 + 1) * 4 * P], KV[(n - 1) % 2][0:w, :], ACT.Copy).then_inc(S.y_copied, 1)

        @block.vector
        def _(dve):
            k = Counts("dve")

            def own(ins):
                ins.then_inc(S.dve_step, 1)
                k.add("step")

            def settle():
                wait(dve, S.dve_step, k.now("step"))

            def tile():
                s = k.slot("tile", 2)
                wait(dve, tile_done, k.next("tile"))
                return s

            def refine(v, g, tmp):
                wait(dve, S.root_ready, k.next("root"))
                own(dve.tensor_tensor(tmp, g, g, ALU.mult))
                settle()
                own(dve.tensor_tensor(tmp, tmp, v, ALU.mult))
                settle()
                own(dve.tensor_scalar(tmp, tmp, -0.5, 1.5, ALU.mult, ALU.add))
                settle()
                own(dve.tensor_tensor(g, g, tmp, ALU.mult))
                settle()

            def scale_tokens(b0, blocks):
                for _ in blocks:
                    wait(dve, S.tok_squared, k.next("sq"))
                b1 = b0 + len(blocks)
                dve.tensor_scalar(small[:, 5 + b0:5 + b1], small[:, b0:b1], 1.0 / D, EPS, ALU.mult, ALU.add).then_inc(S.mean_ready, 1)
                refine(small[:, 5 + b0:5 + b1], small[:, 10 + b0:10 + b1], small[:, b0:b1])
                for b, n in enumerate(blocks, b0):
                    tok = mtok[:, b, :] if b < 2 else xtok[0:n, b - 2, :]
                    dve.tensor_scalar(tok, tok, small[0:n, 10 + b:11 + b], None, ALU.mult).then_inc(S.tok_scaled, 1)

            dve.memset(small[:], 1.0).then_inc(S.small_cleared, 1)
            scale_tokens(0, (P, P))
            dve.wait_ge(S.par_ready, 1)
            for r in range(KT // 2):
                dve.wait_ge(S.tok_high, r + 1)
                for t in range(2):
                    ins = dve.scalar_tensor_tensor(mL[:, 2 * r + t, :], RB[r % 4][:, t * M:(t + 1) * M], pcol("mem", 2 * r + t),
                                                   mH[:, 2 * r + t, :].bitcast(F32), ALU.mult, ALU.subtract)
                ins.then_inc(S.tok_low, 1)
            l0, l1, top = pcol("lb0", 0, KT), pcol("lb1", 0, KT), small[:, 16:32]
            own(dve.tensor_tensor(top, l0, l1, ALU.max))
            settle()
            own(dve.tensor_tensor(small[:, 32:48], l0, top, ALU.subtract))
            dve.tensor_tensor(small[:, 48:64], l1, top, ALU.subtract).then_inc(S.lb_shifted, 1)
            dve.wait_ge(S.lb_exp, 1)
            own(dve.tensor_tensor(top, small[:, 32:48], small[:, 48:64], ALU.add))
            settle()
            own(dve.reciprocal(top, top))
            settle()
            own(dve.tensor_tensor(lb[:], small[:, 32:48], top, ALU.mult))
            settle()
            own(dve.tensor_scalar(oml[:], lb[:], -1.0, 1.0, ALU.mult, ALU.add))
            scale_tokens(2, (P, P, NS))
            for t in range(KT):
                dve.wait_ge(S.tok_high, KT // 2 + t + 1)
                dve.scalar_tensor_tensor(hL[:, t, :], RB[t % 4][:, 0:NT], pcol("mix", t), hH[:, t, :].bitcast(F32),
                                         ALU.mult, ALU.subtract).then_inc(S.tok_low, 1)
            k.add("tile", 34)
            for s in range(2):
                dve.wait_ge(mem_out[s], 8 * 16)
            dve.wait_ge(tile_done, 34)
            own(dve.memset(bd[:], 0.0))
            own(dve.memset(bds[:], 0.0))

            def chunks(ap):
                return ap[:, 0:NP].rearrange("p (n c) -> p n c", c=C), ap[:, NP:NT].rearrange("p (n c) -> p n c", c=L)

            def decays():
                for j in range(2):
                    own(dve.tensor_tensor_scan(cum[:, j, :], keep[:], e1[:, j, :], 0.0, ALU.mult, ALU.add))
                settle()
                for j in range(2):
                    c, _ = chunks(cum[:, j, :])
                    o, _ = chunks(cmid[:, j, :])
                    dve.tensor_tensor(o, c, c[:, :, C // 2 - 1:C // 2].to_broadcast([P, NC, C]), ALU.subtract)
                dve.tensor_copy(cmid[:, :, NP:NT], cum[:, :, NP:NT]).then_inc(S.decay_ready, 1)

            def decayed():
                own(dve.tensor_tensor(ki[:], ki[:], e2[:], ALU.mult))
                own(dve.tensor_tensor(qd[:], qd[:], e1[:], ALU.mult))
                settle()
                for j in range(2):
                    kp, ks = chunks(ki[:, j, :])
                    op, os = chunks(ke[:, j, :])
                    ep, es = chunks(e1[:, j, :])
                    dve.tensor_tensor(op, kp, ep[:, :, C - 1:C].to_broadcast([P, NC, C]), ALU.mult)
                    dve.tensor_tensor(os, ks, es[:, :, L - 1:L].to_broadcast([P, B, L]), ALU.mult)
                for j in range(2):
                    qp, _ = chunks(qd[:, j, :])
                    ins = dve.tensor_tensor(qi[:, j, :].rearrange("p (n c) -> p n c", c=C), qp,
                                            emid[:, j, :].rearrange("p (n o) -> p n o", o=1).to_broadcast([P, NC, C]), ALU.mult)
                ins.then_inc(S.prep_ready, 1)

            def own_keys():
                k.add("turned", 2)
                wait(dve, S.turn_copied, k.now("turned"))
                dve.tensor_tensor(kmask[:], ktok[0:NS, 2:3, :].to_broadcast([NS, B, 2 * P]),
                                  own8[:].rearrange("p (b o) -> p b o", o=1).to_broadcast([NS, B, 2 * P]), ALU.mult).then_inc(S.kmask_ready, 1)

            def keep_scores(heads):
                wait(dve, S.scores_done, k.next("scores"))
                dve.memset(small[:, 15:16], 0.0)
                for j in range(heads):
                    for blk in range(2):
                        dve.copy_predicated(bd[:, j, blk * P:(blk + 1) * P], causal[:].bitcast(U32), KV[j][:, blk * P:(blk + 1) * P])
                    ins = dve.copy_predicated(bds[:, j, :], causal8[:].bitcast(U32), KV[j][0:NS, NP:NT])
                ins.then_inc(S.scores_kept, 1)

            def updates(chunk_range, wide):
                for n in chunk_range:
                    for u in range(2):
                        wait(dve, S.kv_done, k.next("kv"))
                        new, old = sp[(n + 1) % 2][:, u, 0:wide], sp[n % 2][:, u, 0:wide]
                        if n == 0:
                            ins = dve.tensor_copy(new, KV[u][:, 0:wide])
                        else:
                            if n > 1:
                                wait(dve, S.inter_done, k.now("inter") + (n - 1))
                            elif u == 0:
                                wait(dve, S.pstate_out, k.now("pstate", 0, 16))
                            wait(dve, S.state_ready, k.now("st", 1))
                            ins = dve.scalar_tensor_tensor(new, old, elast[:, u, n:n + 1], KV[u][:, 0:wide], ALU.mult, ALU.add)
                        ins.then_inc(S.state_ready, 1)
                        k.add("st")

            def sample_updates(bs, heads, slot=None):
                for b in bs:
                    for u in range(2):
                        wait(dve, S.kv_done, k.next("kv"))
                        c = NP + b * L + L - 1
                        state = s0h[slot][:, b, u, :] if heads == 2 else s0g[b % 4][:, u, :]
                        dve.scalar_tensor_tensor(state, state, e1[:, u, c:c + 1], KV[u][:, 0:(P if heads == 2 else GV)],
                                                 ALU.mult, ALU.add).then_inc(S.sample_ready, 1)
                        k.add("sample_ready")

            def sigmoid(buf):
                own(dve.tensor_scalar(buf, buf, 1.0, None, ALU.add))
                settle()
                own(dve.reciprocal(buf, buf))
                settle()

            def silu_gate(v):
                s = tile()
                wait(dve, S.gate_exp, k.next("gate"))
                sigmoid(ge[s][:])
                dve.tensor_tensor(gate[:, v, :], PB[s][:, 0:NT], ge[s][:], ALU.mult).then_inc(bank_free[s], 1)

            def mix_gate(v):
                s = tile()
                wait(dve, S.gate_exp, k.next("gate"))
                own(dve.tensor_scalar(ge[s][:], ge[s][:], 1.0, None, ALU.add))
                settle()
                own(dve.reciprocal(ge[s][:], ge[s][:]))
                settle()
                dve.tensor_tensor(gate[:, v, :], gate[:, v, :], ge[s][:], ALU.mult).then_inc(bank_free[s], 1)

            with k.turns(dve, "gla", GH) as h:
                for j in range(2):
                    wait(dve, S.abs_ready, k.next("abs"))
                    dve.tensor_scalar(cmid[:, j, :], T[j][:, 0:NT], pcol("ba", h * 2 + j), 0.0, ALU.add, ALU.min).then_inc(S.alog_used, 1)
                wait(dve, S.alog_used, k.now("abs"))
                wait(dve, S.ln_ready, k.next("ln"))
                own(dve.tensor_tensor(e1[:], cmid[:], e1[:], ALU.subtract))
                settle()
                own(dve.tensor_scalar(e1[:], e1[:], 1.0 / 16.0, None, ALU.mult))
                settle()
                decays()
                wait(dve, S.exps_ready, k.next("exps"))
                k.add("tile", 4)
                for s in range(2):
                    wait(dve, bank_free[s], k.rounds("tile", 2))
                decayed()
                k.add("tile", 4)
                own_keys()
                keep_scores(1)
                k.add("turned", 4)
                silu_gate(0)
                updates(range(3), GV)
                silu_gate(1)
                updates(range(3, 6), GV)
                silu_gate(2)
                updates(range(6, NC), GV)
                k.add("inter", NC - 1)
                k.add("pstate")
                sample_updates(range(1), 1)
                silu_gate(3)
                sample_updates(range(1, 4), 1)
                mix_gate(0)
                mix_gate(1)
                sample_updates(range(4, 6), 1)
                mix_gate(2)
                sample_updates(range(6, 8), 1)
                wait(dve, S.sample_ready, k.now("sample_ready"))
                wait(dve, S.ss_done, k.next("ss"))
                dve.tensor_scalar(rsg[:, 0, :], O[1][:, 0:NT], 1.0 / GV, EPS, ALU.mult, ALU.add).then_inc(S.ss_used, 1)
                wait(dve, S.ss_used, k.now("ss"))
                dve.tensor_copy(small[:, 15:16], rsg[:, 0, 0:1]).then_inc(S.mean_ready, 1)
                mix_gate(3)
                refine(rsg[:, 0, :], sqg[:, 0, :], tmpg[:, 0, :])
                for v in range(4):
                    own(dve.scalar_tensor_tensor(tmpg[:, v % 2, :], vo[:, v, :], pcol("glan", h * 4 + v), sqg[:, 0, :], ALU.mult, ALU.mult))
                    settle()
                    ins = dve.tensor_tensor(omix[:, ds(h * 4 + v, 1), :].rearrange("p a n -> p (a n)"), tmpg[:, v % 2, :], gate[:, v, :], ALU.mult)
                    if v < 3:
                        own(ins)
                ins.then_inc(S.mixed, 1)
                k.add("mixed")

            def hgrn_pair(pair, sub):
                for j in range(2):
                    s = tile()
                    wait(dve, S.f_exp, k.next("f_exp"))
                    dve.tensor_scalar(e1[:, j, :], e1[:, j, :], 1.0, None, ALU.add).then_inc(bank_free[s], 1)
                    wait(dve, bank_free[s], k.rounds("tile", 2, 1, more=1))
                    own(dve.reciprocal(e1[:, j, :], e1[:, j, :]))
                    settle()
                    own(dve.tensor_scalar(cum[:, j, :], e1[:, j, :], oml[:, ds(pair * 2 + j, 1)], lb[:, ds(pair * 2 + j, 1)], ALU.mult, ALU.add))
                    settle()
                    ins = dve.tensor_scalar(ki[:, j, :], cum[:, j, :], -1.0, 1.0, ALU.mult, ALU.add)
                    if j == 0:
                        own(ins)
                ins.then_inc(S.f_ready, 1)
                k.add("f_ready")

                def query(j):
                    s = tile()
                    wait(dve, S.gate_exp, k.next("gate"))
                    sigmoid(e2[:, j, :])
                    dve.scalar_tensor_tensor(qd[:, j, :], PB[s][:, 0:NT], P ** -0.5, e2[:, j, :], ALU.mult, ALU.mult).then_inc(bank_free[s], 1)
                query(0)
                wait(dve, S.ln_ready, k.next("ln"))
                for j in range(2):
                    own(dve.tensor_tensor_scan(cum[:, j, :], keep[:], e1[:, j, :], 0.0, ALU.mult, ALU.add))
                settle()
                for j in range(2):
                    c, _ = chunks(cum[:, j, :])
                    o, _ = chunks(cmid[:, j, :])
                    own(dve.tensor_tensor(o, c, c[:, :, C // 2 - 1:C // 2].to_broadcast([P, NC, C]), ALU.subtract))
                query(1)
                dve.tensor_copy(cmid[:, :, NP:NT], cum[:, :, NP:NT]).then_inc(S.decay_ready, 1)
                wait(dve, S.exps_ready, k.next("exps"))
                wait(dve, S.f_ready, k.now("f_ready"))
                for s in range(2):
                    wait(dve, bank_free[s], k.rounds("tile", 2))
                decayed()
                k.add("tile", 2)
                own_keys()
                keep_scores(2)
                k.add("turned", 2)
                silu_gate(0)
                updates(range(NC), P)
                k.add("inter", NC - 1)
                k.add("pstate")
                silu_gate(1)
                sample_updates(range(B), 2, sub)
                mix_gate(0)
                wait(dve, S.sample_ready, k.now("sample_ready"))
                wait(dve, S.ss_done, k.next("ss"))
                own(dve.tensor_scalar(rsg[:, 0, :], O[0][:, 0:NT], 1.0 / P, EPS, ALU.mult, ALU.add))
                dve.tensor_scalar(rsg[:, 1, :], O[1][:, 0:NT], 1.0 / P, EPS, ALU.mult, ALU.add).then_inc(S.ss_used, 1)
                wait(dve, S.ss_used, k.now("ss"))
                settle()
                dve.tensor_copy(small[:, 15:16], rsg[:, 0, 0:1]).then_inc(S.mean_ready, 1)
                mix_gate(1)
                refine(rsg[:], sqg[:, 0:2, :], tmpg[:])
                for j in range(2):
                    own(dve.scalar_tensor_tensor(tmpg[:, j, :], vo[:, j, :], pcol("hgn", pair * 2 + j), sqg[:, j, :], ALU.mult, ALU.mult))
                settle()
                own(dve.tensor_tensor(tmpg[:], tmpg[:], gate[:, 0:2, :], ALU.mult))
                settle()
                wait(dve, S.mixed, k.now("mixed"))
                om = omix[:, ds(pair * 2, 2), :]
                dve.tensor_tensor(om, om, tmpg[:], ALU.add).then_inc(S.mixed, 1)
                k.add("mixed")

            with k.turns(dve, "hgrn", HH // 4) as i:
                hgrn_pair(i * 2, 0)
                hgrn_pair(i * 2 + 1, 1)

            for g in range(4):
                c = slice(4 * g, 4 * g + 4)
                dve.wait_ge(S.mix_high, g + 1)
                dve.tensor_tensor(hL[:, c, :], omix[:, c, :], hH[:, c, :].bitcast(F32), ALU.subtract).then_inc(S.mix_split, 1)

            own(dve.memset(acc[:], 0.0))

            def add_square(s, sem=None):
                wait(dve, S.sq_ready, k.next("sqr"))
                settle()
                own(dve.tensor_tensor(acc[:], acc[:], sq[s][:], ALU.add))

            def residual_tile(i, t, first=False, square=True):
                s = tile()
                xt = x[:, ds(i * 4 + t, 1), :].rearrange("p a n -> p (a n)")
                if first:
                    dve.tensor_copy(xt, PB[s][:, 0:NT]).then_inc(bank_free[s], 1)
                else:
                    dve.tensor_tensor(xt, xt, PB[s][:, 0:NT], ALU.add).then_inc(bank_free[s], 1)
                if square:
                    add_square(s)

            def norm_scale():
                settle()
                dve.tensor_copy(acc[:], acc[:]).then_inc(S.acc_ready, 1)
                wait(dve, S.sum_done, k.next("sum"))
                dve.tensor_scalar(rs[:], T[0][:, 0:NT], 1.0 / D, EPS, ALU.mult, ALU.add).then_inc(S.mean_ready, 1)
                wait(dve, S.root_ready, k.now("root", -1))
                refine(rs[:], sq[0][:], sq[1][:])
                own(dve.memset(acc[:], 0.0))

            def norm_tiles(gain):
                def low(g):
                    wait(dve, S.norm_high, k.next("norm_high"))
                    dve.tensor_tensor(hL[:, 4 * g:4 * g + 4, :], nrm[g % 2][:], hH[:, 4 * g:4 * g + 4, :].bitcast(F32),
                                      ALU.subtract).then_inc(S.normed, 1)
                    k.add("normed")
                for g in range(4):
                    if g >= 2:
                        wait(dve, S.normed, k.now("normed"))
                    for t in range(4):
                        ins = dve.scalar_tensor_tensor(nrm[g % 2][:, t, :], x[:, 4 * g + t, :], pcol(gain, 4 * g + t), sq[0][:], ALU.mult, ALU.mult)
                    ins.then_inc(S.norm_tmp, 1)
                    if g:
                        wait(dve, S.norm_tmp, k.now("tmp"))
                        low(g - 1)
                    k.add("tmp")
                wait(dve, S.norm_tmp, k.now("tmp"))
                low(3)

            dve.wait_ge(S.x_in, 64)
            def stage(i, t):
                s = t % 2
                own(dve.tensor_copy(xst[s][:, 0:2, :], xres[:, 0:2, ds((i * 4 + t) * P, P)]))
                dve.tensor_copy(xst[s][0:NS, 2, :], xres[0:NS, 2, ds((i * 4 + t) * P, P)]).then_inc(S.xst_ready, 1)
            stage(0, 0)
            stage(0, 1)
            with k.turns(dve, "wout", 3) as i:
                for t in range(4):
                    residual_tile(i, t, first=True)
                    stage(i, t + 2)
            for t in range(4):
                residual_tile(3, t, first=True)
                if t < 2:
                    stage(3, t + 2)
            norm_scale()
            norm_tiles("xat")
            k.add("tile", 16)

            def copy_keys(h):
                k.add("kturn")
                s = k.slot("kturn", 4)
                wait(dve, S.k_turned, k.now("kturn", -1))
                dve.tensor_copy(kT[:, h, 2:4, :], RB[s][:].rearrange("p (t n) -> p t n", t=2)).then_inc(S.kT_odd, 1)
                k.add("kturn")

            def low_part(dst_h, dst_l, bank, sem):
                dve.tensor_tensor(dst_l, bank, dst_h.bitcast(F32), ALU.subtract).then_inc(sem, 1)

            for h in range(MH):
                copy_keys(h)
                dve.wait_ge(S.sp_done, h + 1)
                own(dve.tensor_reduce(small[:, 0:2], T[0][:].rearrange("p (l m) -> p l m", l=2), AX.X, ALU.max))
                settle()
                dve.tensor_scalar(small[:, 2:4], small[:, 0:2], -1.0, None, ALU.mult).then_inc(S.pmax_ready, 1)
                dve.wait_ge(S.pp_exp, h + 1)
                own(dve.reciprocal(small[:, 6:8], small[:, 4:6]))
                settle()
                own(dve.tensor_scalar(pP[:, 0, :], pP[:, 0, :], small[:, 6:7], None, ALU.mult))
                dve.tensor_scalar(pP[:, 1, :], pP[:, 1, :], small[:, 7:8], None, ALU.mult).then_inc(S.pp_ready, 1)
                for dt in range(4):
                    n = 4 * h + dt
                    dve.wait_ge(S.mop_high, n + 1)
                    low_part(hH[:, n, 0:NP], hL[:, n, 0:NP], PB[n % 2][:, 0:NP], S.mop_split)
            with k.turns(dve, "xattn", B) as b:
                for h in range(MH):
                    copy_keys(h)
                wait(dve, S.s_done, k.next("smp"))
                own(dve.tensor_reduce(small[0:32, 8:9], T[1][0:32, 0:M], AX.X, ALU.max))
                settle()
                dve.tensor_scalar(small[0:32, 9:10], small[0:32, 8:9], -1.0, None, ALU.mult).then_inc(S.max_ready, 1)
                wait(dve, S.p_exp, k.now("smp"))
                own(dve.reciprocal(small[0:32, 11:12], small[0:32, 10:11]))
                settle()
                dve.tensor_scalar(pr[:], pr[:], small[0:32, 11:12], None, ALU.mult).then_inc(S.p_ready, 1)
                wait(dve, S.mo_high, k.now("smp"))
                cols = ds(b * L + NP, L)
                low_part(hH[:, :, cols], hL[:, :, cols], PB[0][:, 0:P].rearrange("p (t n) -> p t n", t=KT), S.mo_split)
            own(dve.memset(acc[:], 0.0))
            with k.turns(dve, "memo", 4) as i:
                for t in range(4):
                    residual_tile(i, t)
            norm_scale()
            norm_tiles("ffn")

            own(dve.memset(seq[0][:, 0:2], 0.0))
            own(dve.memset(seq[1][:, 0:2], 0.0))
            settle()

            def up(j, col, js, last4):
                wait(dve, S.seq_ready, k.next("conv"))
                own(dve.tensor_scalar(cv[js][:, 0:NCONV], seq[js][:, 0:NCONV], pcol("cw0", j), pcol("cb", j), ALU.mult, ALU.add))
                settle()
                own(dve.scalar_tensor_tensor(cv[js][:, 0:NCONV], seq[js][:, 1:1 + NCONV], pcol("cw1", j), cv[js][:, 0:NCONV], ALU.mult, ALU.add))
                settle()
                dve.scalar_tensor_tensor(cv[js][:, 0:NCONV], seq[js][:, 2:2 + NCONV], pcol("cw2", j), cv[js][:, 0:NCONV], ALU.mult, ALU.add).then_inc(S.conv_ready, 1)
                own(dve.tensor_copy(cnew[:, ds(j, 1), 0:2].rearrange("p a n -> p (a n)"), seq[js][:, NP:NP + 2]))
                smp = seq[js][:, 2 + NP:NSEQ].rearrange("p (b n) -> p b n", b=B)
                dve.tensor_copy(cnew[:, ds(j, 1), 2:18].rearrange("p a (b n) -> p (a b) n", b=B), smp[:, :, L:L + 2]).then_inc(S.ug_kept, 1)
                k.add("tile")
                wait(dve, S.ce_ready, k.now("conv"))
                sigmoid(ce[js][:, 0:NCONV])
                own(dve.tensor_tensor(cv[js][:, 0:NCONV], cv[js][:, 0:NCONV], ce[js][:, 0:NCONV], ALU.mult))
                settle()
                s = tile()
                own(dve.tensor_tensor(av[js][:, 0:NP], cv[js][:, 0:NP], PB[s][:, 0:NP], ALU.mult))
                csm = cv[js][:, 2 + NP:2 + NP + B * (L + 2)].rearrange("p (b n) -> p b n", b=B)[:, :, 0:L]
                dve.tensor_tensor(av[js][:, NP:NT].rearrange("p (b n) -> p b n", b=B), csm,
                                  PB[s][:, NP:NT].rearrange("p (b n) -> p b n", b=B), ALU.mult).then_inc(bank_free[s], 1)
                wait(dve, bank_free[s], k.rounds("tile", 2, 1, more=1))
                settle()
                dve.tensor_copy(av[js][:, 0:1], av[js][:, 0:1]).then_inc(S.av_ready, 1)
                wait(dve, S.act_high, k.now("conv"))
                aht = aH[:, ds(col, 1), :].rearrange("p a n -> p (a n)")
                alt = aL[:, ds(col, 1), :].rearrange("p a n -> p (a n)")
                ins = dve.tensor_tensor(alt, av[js][:], aht.bitcast(F32), ALU.subtract)
                if last4:
                    ins.then_inc(S.act4, 1)
                else:
                    own(ins)

            for g, (j0, nk) in enumerate(GROUPS):
                with k.turns(dve, f"up{g}", nk // 4) as i:
                    for t in range(4):
                        up(i * 4 + (j0 + t), i * 4 + t, t % 2, t == 3)
                for t in range(nk % 4):
                    up(j0 + nk // 4 * 4 + t, nk // 4 * 4 + t, t % 2, t == nk % 4 - 1)
                with k.turns(dve, f"down{g}", 4) as i:
                    for t in range(4):
                        residual_tile(i, t, square=g == 2)
            norm_scale()
            for g in range(4):
                for t in range(4):
                    ins = dve.scalar_tensor_tensor(x[:, 4 * g + t, :], x[:, 4 * g + t, :], pcol("fin", 4 * g + t), sq[0][:], ALU.mult, ALU.mult)
                ins.then_inc(S.y_normed, 1)


_INS = ["x_prompt", "x_sample", "mem_prompt", "state_gla", "state_hgrn", "state_ffn_conv", "cache_mem_k", "cache_mem_v",
        "norm_mix_g", "w_in", "gla_w_a_up", "gla_b_a", "gla_norm_g", "hgrn_lower_bound", "hgrn_norm_g", "w_out",
        "norm_xattn_g", "norm_mem_g", "w_mem_q", "w_mem_k", "w_mem_v", "w_mem_o", "norm_ffn_g", "w_ffn_up",
        "ffn_conv_w", "ffn_conv_b", "w_ffn_down", "norm_final_g"]
_OUTS = {"y_p": (1, NP, D), "y_s": (B, L, D), "gla_p": (1, 1, GH, GK, GV), "hgrn_p": (1, 1, HH, P, P),
         "conv_p": (1, 1, 2, FF), "mem_k": (1, 1, M, MH, MD), "mem_v": (1, 1, M, MH, MD),
         "gla_s": (1, B, GH, GK, GV), "hgrn_s": (1, B, HH, P, P), "conv_s": (1, B, 2, FF)}


def kernel(**inputs):
    import numpy as _np
    import concourse.bacc as _bacc
    from concourse.bass_utils import run_bass_kernel_spmd as _run

    nc = _bacc.Bacc("TRN2", target_bir_lowering=False, num_devices=1)
    arrays, ins, outs = {}, {}, {}
    for name in _INS:
        arr = _np.ascontiguousarray(inputs[name])
        arrays[f"in_{name}"] = arr
        ins[name] = nc.dram_tensor(f"in_{name}", arr.shape, mybir.dt.from_np(arr.dtype), kind="ExternalInput").ap()
    for name, shape in _OUTS.items():
        outs[name] = nc.dram_tensor(f"out_{name}", shape, F32, kind="ExternalOutput").ap()
    build(nc, ins, outs)
    r = _run(nc, [arrays], core_ids=[0])
    return tuple(r.results[0][f"out_{name}"] for name in _OUTS)
```

```python
from contextlib import ExitStack, contextmanager

import concourse.bass as bass
from concourse import mybir

F32 = mybir.dt.float32
F32R = mybir.dt.float32r
U32 = mybir.dt.uint32
ALU = mybir.AluOpType
ACT = mybir.ActivationFunctionType
AX = mybir.AxisListType
ds = bass.ds

P = 128
D = 2048
KT = D // P
NP, B, L = 256, 8, 8
NS = B * L
NT = NP + NS
M = 256
FF = 5504
FT = FF // P
GH, GK, GV = 4, 256, 512
HH = 16
MH, MD = 4, 512
C = 32
NC = NP // C
CPB = P // C
EPS = 1e-6
NSEQ = NP + 2 + B * (L + 2)
NCONV = NSEQ - 2

ARENA = 96 * 1024 + 256
GROUPS = ((0, 16), (16, 16), (32, FT - 32))
CPART = 24
GQ, GKC = 0, GH * GK
GVC = GKC + GH * GK
GG = GVC + GH * GV
GA = GG + GH * GV
HQ = GA + 16
HF, HI, HG = HQ + D, HQ + 2 * D, HQ + 3 * D
MA, MB = HQ + 4 * D, HQ + 5 * D

PAR = {}
_at = 0
for _name, _rows in (("mix", KT), ("ba", 8), ("glan", KT), ("lb0", KT), ("lb1", KT), ("hgn", KT), ("xat", KT), ("mem", KT),
                     ("ffn", KT), ("fin", KT), ("cw0", FT), ("cw1", FT), ("cw2", FT), ("cb", FT)):
    if _at // P != (_at + _rows - 1) // P:
        _at = (_at // P + 1) * P
    PAR[_name] = (_at, _rows)
    _at += _rows
PBLK = (_at + P - 1) // P

PER = {('act', 'down0'): {'ahead': 4, 'tile': 4},
 ('act', 'down1'): {'ahead': 4, 'tile': 4},
 ('act', 'down2'): {'ahead': 4, 'tile': 4},
 ('act', 'gla'): {'ahead': 16,
                  'alog': 2,
                  'decay': 1,
                  'inter': 7,
                  'mix': 1,
                  'o': 1,
                  'root': 1,
                  'step': 2,
                  'tile': 16,
                  'turned': 6},
 ('act', 'hgrn'): {'ahead': 20,
                   'decay': 2,
                   'f': 2,
                   'mix': 2,
                   'o': 2,
                   'o_copied': 4,
                   'root': 2,
                   'step': 2,
                   'tile': 20,
                   'turned': 8},
 ('act', 'mem_v'): {'ahead': 4, 'memo0': 1, 'memo1': 1, 'memturn': 4, 'tile': 4},
 ('act', 'memo'): {'ahead': 4, 'tile': 4},
 ('act', 'memq'): {'ahead': 4, 'tile': 4},
 ('act', 'up0'): {'ahead': 4, 'conv': 2, 'tile': 4},
 ('act', 'up1'): {'ahead': 4, 'conv': 2, 'tile': 4},
 ('act', 'up2'): {'ahead': 4, 'conv': 2, 'tile': 4},
 ('act', 'wout'): {'ahead': 4, 'tile': 4},
 ('act', 'xattn'): {'kturn': 8, 'max': 1, 'smp': 1},
 ('dve', 'down0'): {'tile': 4},
 ('dve', 'down1'): {'tile': 4},
 ('dve', 'down2'): {'sqr': 4, 'step': 4, 'tile': 4},
 ('dve', 'gla'): {'abs': 2,
                  'exps': 1,
                  'gate': 8,
                  'inter': 7,
                  'kv': 32,
                  'ln': 1,
                  'mixed': 1,
                  'pstate': 1,
                  'root': 1,
                  'sample_ready': 16,
                  'scores': 1,
                  'ss': 1,
                  'st': 16,
                  'step': 32,
                  'tile': 16,
                  'turned': 6},
 ('dve', 'hgrn'): {'exps': 2,
                   'f_exp': 4,
                   'f_ready': 2,
                   'gate': 12,
                   'inter': 14,
                   'kv': 64,
                   'ln': 2,
                   'mixed': 2,
                   'pstate': 2,
                   'root': 2,
                   'sample_ready': 32,
                   'scores': 2,
                   'ss': 2,
                   'st': 32,
                   'step': 60,
                   'tile': 20,
                   'turned': 8},
 ('dve', 'memo'): {'gained': 4, 'sqr': 4, 'step': 4, 'tile': 4},
 ('dve', 'memq'): {'tile': 4},
 ('dve', 'up0'): {'conv': 4, 'step': 39, 'tile': 8},
 ('dve', 'up1'): {'conv': 4, 'step': 39, 'tile': 8},
 ('dve', 'up2'): {'conv': 4, 'step': 39, 'tile': 8},
 ('dve', 'wout'): {'gained': 4, 'sqr': 4, 'step': 8, 'tile': 4},
 ('dve', 'xattn'): {'kturn': 8, 'queries': 1, 'smp': 1, 'step': 6, 'v_used': 4},
 ('pe', 'down0'): {'tile': 4},
 ('pe', 'down1'): {'tile': 4},
 ('pe', 'down2'): {'tile': 4},
 ('pe', 'gla'): {'o': 3,
                 'prep': 1,
                 's0_in0': 2,
                 's0_in1': 2,
                 's0_in2': 2,
                 's0_in3': 2,
                 'sample_ready': 16,
                 'ss': 1,
                 'state_ready': 16,
                 'tile': 16,
                 'turned': 6,
                 'wa': 1},
 ('pe', 'hgrn'): {'o': 4,
                  'pair': 2,
                  'prep': 2,
                  's0_in0': 2,
                  's0_in1': 2,
                  'sample_ready': 32,
                  'ss': 2,
                  'state_ready': 32,
                  'tile': 20,
                  'turned': 8},
 ('pe', 'mem_k'): {'memturn': 4, 'tile': 4},
 ('pe', 'mem_v'): {'memturn': 4, 'tile': 4},
 ('pe', 'memo'): {'tile': 4},
 ('pe', 'memq'): {'tile': 4},
 ('pe', 'up0'): {'tile': 4},
 ('pe', 'up1'): {'tile': 4},
 ('pe', 'up2'): {'tile': 4},
 ('pe', 'wout'): {'tile': 4, 'xst': 4},
 ('pe', 'xattn'): {'kc0': 1,
                   'kc1': 1,
                   'kc2': 1,
                   'kc3': 1,
                   'kturn': 4,
                   'scored': 1,
                   'smp': 1,
                   'vc0': 1,
                   'vc1': 1,
                   'vc2': 1,
                   'vc3': 1},
 ('pool', 'split'): {'tile': 4},
 ('sp', 'down0'): {'load': 2},
 ('sp', 'down1'): {'load': 2},
 ('sp', 'down2'): {'load': 2},
 ('sp', 'gla'): {'load': 8,
                 's0_out0': 2,
                 's0_out1': 2,
                 's0_out2': 2,
                 's0_out3': 2,
                 'sample_ready': 16,
                 'state_ready': 16,
                 'wa': 1},
 ('sp', 'hgrn'): {'load': 10, 's0_out0': 2, 's0_out1': 2, 'sample_ready': 32, 'state_ready': 32},
 ('sp', 'mem_k'): {'load': 2},
 ('sp', 'mem_v'): {'load': 2},
 ('sp', 'memo'): {'load': 2},
 ('sp', 'memq'): {'load': 2},
 ('sp', 'up0'): {'load': 2},
 ('sp', 'up1'): {'load': 2},
 ('sp', 'up2'): {'load': 2},
 ('sp', 'wout'): {'load': 2},
 ('sp', 'xattn'): {'k_turned': 8, 'v_used': 4}}


class Counts:

    def __init__(self, who):
        self.who, self.n, self.per, self.i = who, {}, {}, None

    def add(self, name, k=1):
        self.n[name] = self.n.get(name, 0) + k

    def now(self, name, lag=0, unit=1):
        n, per = self.n.get(name, 0) - lag, self.per.get(name, 0)
        if self.i is None or not per:
            return n * unit
        assert n >= 0, (self.who, name, n)
        return self.i * (per * unit) + n * unit

    def next(self, name, unit=1):
        self.add(name)
        return self.now(name, 0, unit)

    def slot(self, name, k):
        assert self.per.get(name, 0) % k == 0, (self.who, name, self.per.get(name), k)
        return self.n.get(name, 0) % k

    def rounds(self, name, k, lag=0, unit=1, more=0):
        n, per = (self.n.get(name, 0) - lag) // k + more, self.per.get(name, 0) // k
        if self.i is None or not per:
            return n * unit
        assert n >= 0, (self.who, name, n)
        return self.i * (per * unit) + n * unit

    @contextmanager
    def turns(self, eng, name, n):
        per = PER.get((self.who, name), {})
        start = dict(self.n)
        with eng.Fori(0, n) as i:
            self.i, self.per = i, per
            yield i
            grown = {k: v - start.get(k, 0) for k, v in self.n.items() if v != start.get(k, 0)}
            assert grown == per, (self.who, name, grown, per)
        self.i, self.per = None, {}
        self.n = {k: start.get(k, 0) + grown.get(k, 0) * n for k in self.n}


def wait(eng, sem, value):
    if not (isinstance(value, int) and value <= 0):
        eng.wait_ge(sem, value)


def build(nc, a, out):
    ctx = ExitStack()
    with ctx:
        sems = {}

        class Sems:
            def __getattribute__(self, name):
                if name not in sems:
                    sems[name] = ctx.enter_context(nc.semaphore(name))
                return sems[name]
        S = Sems()

        def sb(name, shape, dt=F32):
            return ctx.enter_context(nc.sbuf_tensor(name, shape, dt))

        raw = [sb(f"raw{s}", [P, KT, 2 * P]) for s in range(2)]
        wH = [sb(f"wH{s}", [P, KT, P], F32R) for s in range(2)]
        wL = [sb(f"wL{s}", [P, KT, P], F32R) for s in range(2)]
        hH = sb("hH", [P, KT, NT], F32R)
        hL = sb("hL", [P, KT, NT], F32R)
        ident = sb("ident", [P, P])
        ones = sb("ones", [P, P])
        causal = sb("causal", [P, P])
        causal8 = sb("causal8", [NS, NS])
        own8 = sb("own8", [NS, B])
        keep = sb("keep", [P, NT])
        par = sb("par", [P, PBLK, P])
        lb = sb("lb", [P, KT])
        oml = sb("oml", [P, KT])
        small = sb("small", [P, 64])
        wah = sb("wah", [16, GK])
        gaT = sb("gaT", [16, NT])

        base = nc.sbuf_base
        sb("arena", [P, ARENA // 4])

        def at(name, kb, shape, dt=F32):
            n = 4
            for s in shape[1:]:
                n *= s
            assert kb * 1024 + n <= ARENA, (name, kb * 1024 + n)
            return nc.alloc_sbuf_tensor_at(name, shape, dt, offset=base + int(kb * 1024))

        mtok = at("mtok", 0, [P, 2, D])
        xtok = at("xtok", 16, [P, 3, D])
        mH = at("mH", 40, [P, KT, M], F32R)
        mL = at("mL", 56, [P, KT, M], F32R)
        sqtok = at("sqtok", 72, [P, D])
        memo = [at(f"memo{s}", 80 + 2 * s, [P, 2, 2 * P]) for s in range(2)]
        memf = [at(f"memf{s}", 86 + s, [P, M]) for s in range(2)]
        parrow = at("parrow", 84, [P, PBLK, P])
        omix = at("omix", 0, [P, KT, NT])
        s0g = [at(f"s0g{s}", 20 + 4 * s, [P, 2, GV]) for s in range(4)]
        s0h = [at(f"s0h{s}", 20 + 8 * s, [P, B, 2, P]) for s in range(2)]
        qd = at("qd", 36, [P, 2, NT])
        ki = at("ki", 38.5, [P, 2, NT])
        cum = at("cum", 41, [P, 2, NT])
        cmid = at("cmid", 43.5, [P, 2, NT])
        e1 = at("e1", 46, [P, 2, NT])
        e2 = at("e2", 48.5, [P, 2, NT])
        ke = at("ke", 51, [P, 2, NT])
        qi = at("qi", 53.5, [P, 2, NP])
        vo = at("vo", 55.5, [P, 4, NT])
        vtok = at("vtok", 60.5, [P, 3, GV])
        ktok = at("ktok", 66.5, [P, 3, 2 * P])
        kmask = at("kmask", 69.5, [NS, B, 2 * P])
        sp = [at(f"sp{s}", 77.5 + 4 * s, [P, 2, GV]) for s in range(2)]
        gate = at("gate", 85.5, [P, 4, NT])
        ge = [at(f"ge{s}", 90.5 + 1.25 * s, [P, NT]) for s in range(2)]
        bd = at("bd", 93, [P, 2, NP])
        bds = at("bds", 95, [NS, 2, NS])
        emid = at("emid", 95.5, [P, 2, NC])
        elast = at("elast", 95.5625, [P, 2, NC])
        sqg = at("sqg", 41, [P, 4, NT])
        rsg = at("rsg", 46, [P, 2, NT])
        tmpg = at("tmpg", 48.5, [P, 2, NT])
        x = at("x", 0, [P, KT, NT])
        xres = at("xres", 20, [P, 3, D])
        xst = [at(f"xst{s}", 44 + 1.5 * s, [P, 3, P]) for s in range(2)]
        q = at("q", 20, [P, KT, NT])
        gainedq = at("gainedq", 48, [P, KT, NT])
        gainedf = at("gainedf", 20, [P, KT, NT])
        kc = at("kc", 44, [P, MH, 2, MD])
        vc = at("vc", 60, [P, MH, 2, MD])
        kT = at("kT", 76, [P, 2, 4, M])
        qz = at("qz", 84, [P, KT, 32])
        pz = at("pz", 86, [P, MH, 2, NS])
        mor = at("mor", 76, [NS, D])
        acc = at("acc", 92, [P, NT])
        sq = [at(f"sq{s}", 93.25 + 1.25 * s, [P, NT]) for s in range(2)]
        rs = at("rs", 40, [P, NT])
        pr = at("pr", 92.25, [32, M])
        pP = [at(f"pP{s}", 40 + 2 * s, [P, 2, M]) for s in range(2)]
        pTP = [at("pTP0", 88, [P, 2, NP]), at("pTP1", 90, [P, 2, NP])]
        aH = at("aH", 20, [P, KT, NT], F32R)
        aL = at("aL", 41.5, [P, KT, NT], F32R)
        crow = at("crow", 62, [18, CPART * P])
        crow1 = at("crow1", 41.5, [16, (FT - CPART) * P])
        cin = at("cin", 74, [P, FT, 16])
        cnew = at("cnew", 76.75, [P, FT, 18])
        seq = [at(f"seq{s}", 80 + 1.375 * s, [P, NSEQ]) for s in range(2)]
        cv = [at(f"cv{s}", 82.75 + 1.375 * s, [P, NSEQ]) for s in range(2)]
        ce = [at(f"ce{s}", 85.5 + 1.375 * s, [P, NSEQ]) for s in range(2)]
        av = [at(f"av{s}", 88.25 + 1.25 * s, [P, NT]) for s in range(2)]
        ytok = at("ytok", 42, [P, 3, D])

        ps = [ctx.enter_context(nc.psum_tensor(n, [P, 512], F32)) for n in ("P0", "P1", "T0", "T1", "O0", "O1", "KV0", "KV1")]
        PB, T, O, KV = ps[0:2], ps[2:4], ps[4:6], ps[6:8]
        RB = [O[0], O[1], KV[0], KV[1]]

        def kv_bank(n, u):
            return (KV[u], T[u])[n % 2]

        def pcol(name, t, n=1):
            at0, rows = PAR[name]
            return par[:, at0 // P, ds(at0 % P + t, n)]

        landed = [S.landed0, S.landed1]
        bank_free = [S.bank0_free, S.bank1_free]
        high_ready, low_ready, tile_done = S.high_ready, S.low_ready, S.tile_done
        mem_out = [S.mem_out0, S.mem_out1]
        s0_in = [S.s0_in0, S.s0_in1, S.s0_in2, S.s0_in3]
        s0_out = [S.s0_out0, S.s0_out1, S.s0_out2, S.s0_out3]
        kc_in = [S.kc_in0, S.kc_in1, S.kc_in2, S.kc_in3]
        vc_in = [S.vc_in0, S.vc_in1, S.vc_in2, S.vc_in3]

        w_in = a["w_in"][0]
        w_up = a["w_ffn_up"][0]
        rows_of = lambda ap: ap.rearrange("(t p) n -> p t n", p=P)
        NLOADS = 16 + 1 + 32 + 40 + 8 + 8 + 8 + FT + 24
        NTILES = 2 * NLOADS
        mk_out = out["mem_k"][0, 0].rearrange("(t p) h d -> p t (h d)", p=P)
        mv_out = out["mem_v"][0, 0].rearrange("(t p) h d -> p t (h d)", p=P)

        block = ctx.enter_context(nc.Block())

        @block.sync
        def _(sp_):
            k = Counts("sp")

            def begin_load():
                s = k.slot("load", 2)
                wait(sp_, low_ready, k.now("load", 1, 2))
                k.add("load")
                return s

            def load(w, col, nk=KT):
                s = begin_load()
                half = (nk + 1) // 2
                for lo, hi in ((0, half), (half, nk)):
                    sp_.dma_start(raw[s][:, lo:hi, :], rows_of(w)[:, lo:hi, ds(col, 2 * P)]).then_inc(landed[s], 16)

            sp_.dma_start(mtok[:], a["mem_prompt"][0].rearrange("(b p) d -> p b d", p=P)).then_inc(S.mem_in, 16)
            names = {"mix": a["norm_mix_g"][0], "ba": a["gla_b_a"][0], "glan": a["gla_norm_g"][0],
                     "lb0": a["hgrn_lower_bound"][0], "lb1": a["hgrn_lower_bound"][1], "hgn": a["hgrn_norm_g"][0],
                     "xat": a["norm_xattn_g"][0], "mem": a["norm_mem_g"][0], "ffn": a["norm_ffn_g"][0],
                     "fin": a["norm_final_g"], "cw0": a["ffn_conv_w"][0, 0], "cw1": a["ffn_conv_w"][0, 1],
                     "cw2": a["ffn_conv_w"][0, 2], "cb": a["ffn_conv_b"][0]}
            wait(sp_, S.rows_cleared, 1)
            for n, src in names.items():
                r0, rows = PAR[n]
                sp_.dma_start(parrow[r0 % P:r0 % P + rows, r0 // P, :], src.rearrange("(t p) -> t p", p=P)).then_inc(S.par_in, 16)
            load(a["w_mem_k"][0], 0)
            load(a["w_mem_k"][0], 2 * P)
            sp_.dma_start(xtok[:, 0:2, :], a["x_prompt"][0].rearrange("(b p) d -> p b d", p=P)).then_inc(S.x_in, 16)
            sp_.dma_start(xtok[0:NS, 2, :], a["x_sample"].rearrange("b l d -> (b l) d")).then_inc(S.x_in, 16)
            with k.turns(sp_, "mem_k", 3) as i:
                for s in range(2):
                    load(a["w_mem_k"][0], i * (4 * P) + (2 + s) * 2 * P)
            with k.turns(sp_, "mem_v", 4) as i:
                for s in range(2):
                    load(a["w_mem_v"][0], i * (4 * P) + s * 2 * P)
            load(w_in, GA)
            sg = a["state_gla"][0]

            def s0_load(b, h):
                s = b % 4
                wait(sp_, s0_out[s], k.now(f"s0_out{s}", 0, 16))
                sp_.dma_start(s0g[s][:], sg[b, ds(h, 1)].rearrange("o (t p) v -> p (o t) v", p=P)).then_inc(s0_in[s], 16)

            def s0_store(b, h):
                s = b % 4
                k.add("sample_ready", 2)
                wait(sp_, S.sample_ready, k.now("sample_ready"))
                sp_.dma_start(out["gla_s"][0, b, ds(h, 1)].rearrange("o (t p) v -> p (o t) v", p=P), s0g[s][:]).then_inc(s0_out[s], 16)
                k.add(f"s0_out{s}")

            def gla_head(h, after):
                load(w_in, h * GV + GVC)
                load(w_in, h * GV + GVC + 2 * P)
                for b in range(4):
                    if b == 0:
                        wait(sp_, tile_done, 32)
                    s0_load(b, h)
                for g in (GG, MA):
                    load(w_in, h * GV + g)
                    load(w_in, h * GV + g + 2 * P)
                for b in range(4):
                    s0_store(b, h)
                for b in range(4, 8):
                    s0_load(b, h)
                after()
                for b in range(4, 8):
                    s0_store(b, h)
                k.add("state_ready", 2 * NC)
                wait(sp_, S.state_ready, k.now("state_ready"))
                sp_.dma_start(out["gla_p"][0, 0, ds(h, 1)].rearrange("o (t p) v -> p (o t) v", p=P), sp[0][:]).then_inc(S.pstate_out, 16)

            def gla_qk(h):
                wait(sp_, S.alog_done, k.now("wa", 0, 2))
                sp_.dma_start(wah[:], a["gla_w_a_up"][0][:, ds(h * GK, GK)]).then_inc(S.wa_in, 16)
                k.add("wa")
                load(w_in, h * GK + GQ)
                load(w_in, h * GK + GKC)

            gla_qk(0)
            with k.turns(sp_, "gla", GH - 1) as h:
                gla_head(h, lambda: gla_qk(h + 1))

            sh = a["state_hgrn"][0]

            def hgrn_fqi(p):
                load(w_in, p * (2 * P) + HF)
                load(w_in, p * (2 * P) + HQ)
                load(w_in, p * (2 * P) + HI)

            gla_head(GH - 1, lambda: hgrn_fqi(0))

            def hgrn_pair(p, sub, after):
                wait(sp_, s0_out[sub], k.now(f"s0_out{sub}", 0, 16))
                for s in (2 * sub, 2 * sub + 1):
                    wait(sp_, s0_out[s], 16 * 2 * GH)
                for j in range(2):
                    sp_.dma_start(s0h[sub][:, :, j, :], sh[:, ds(p * 2 + j, 1)].rearrange("b o k v -> k (b o) v")).then_inc(s0_in[sub], 16)
                load(w_in, p * (2 * P) + HG)
                load(w_in, p * (2 * P) + MB)
                after()
                k.add("sample_ready", 2 * B)
                wait(sp_, S.sample_ready, k.now("sample_ready"))
                for j in range(2):
                    sp_.dma_start(out["hgrn_s"][0][:, ds(p * 2 + j, 1)].rearrange("b o k v -> k (b o) v"), s0h[sub][:, :, j, :]).then_inc(s0_out[sub], 16)
                k.add(f"s0_out{sub}", 2)
                k.add("state_ready", 2 * NC)
                wait(sp_, S.state_ready, k.now("state_ready"))
                sp_.dma_start(out["hgrn_p"][0, 0, ds(p * 2, 2)].rearrange("j k v -> k j v"), sp[0][:, :, 0:P]).then_inc(S.pstate_out, 16)

            with k.turns(sp_, "hgrn", HH // 4 - 1) as i:
                hgrn_pair(i * 2, 0, lambda: hgrn_fqi(i * 2 + 1))
                hgrn_pair(i * 2 + 1, 1, lambda: hgrn_fqi(i * 2 + 2))
            last = HH // 2 - 2
            hgrn_pair(last, 0, lambda: hgrn_fqi(last + 1))

            def wout_first():
                load(a["w_out"][0], 0)
                load(a["w_out"][0], 2 * P)
            hgrn_pair(last + 1, 1, wout_first)
            wait(sp_, S.mixed, GH + HH // 2)
            for s in range(2):
                wait(sp_, s0_out[s], k.now(f"s0_out{s}", 0, 16))
            wait(sp_, S.pstate_out, 16 * (GH + HH // 2))
            sp_.dma_start(xres[:, 0:2, :], a["x_prompt"][0].rearrange("(b p) d -> p b d", p=P)).then_inc(S.x_in, 16)
            sp_.dma_start(xres[0:NS, 2, :], a["x_sample"].rearrange("b l d -> (b l) d")).then_inc(S.x_in, 16)
            with k.turns(sp_, "wout", 3) as i:
                for s in range(2):
                    load(a["w_out"][0], i * (4 * P) + (2 + s) * 2 * P)
            with k.turns(sp_, "memq", 4) as i:
                for s in range(2):
                    load(a["w_mem_q"][0], i * (4 * P) + s * 2 * P)
            for s in range(2):
                wait(sp_, mem_out[s], 8 * 16)
            wait(sp_, tile_done, 2 * (16 + 1 + 32 + 40 + 8))
            wait(sp_, S.normed, 4)
            ck, cv_ = a["cache_mem_k"][0], a["cache_mem_v"][0]
            tiles_of = lambda ap: ap.rearrange("(t p) d -> p t d", p=P)
            for h in range(MH):
                sp_.dma_start(kc[:, h], tiles_of(out["mem_k"][0, 0][:, h])).then_inc(kc_in[h], 16)
                sp_.dma_start(vc[:, h], tiles_of(out["mem_v"][0, 0][:, h])).then_inc(vc_in[h], 16)

            def keys(b, h):
                k.add("k_turned", 2)
                wait(sp_, S.k_turned, k.now("k_turned"))
                sp_.dma_start(kc[:, h], ck[ds(b, 1), :, h].rearrange("o (t p) d -> p (o t) d", p=P)).then_inc(kc_in[h], 16)

            def values(b, h):
                wait(sp_, S.v_used, k.next("v_used"))
                sp_.dma_start(vc[:, h], cv_[ds(b, 1), :, h].rearrange("o (t p) d -> p (o t) d", p=P)).then_inc(vc_in[h], 16)

            def keys_and_values(bk, bv):
                keys(bk, 0)
                for h in range(1, MH):
                    keys(bk, h)
                    values(bv, h - 1)
                values(bv, MH - 1)

            load(a["w_mem_o"][0], 0)
            load(a["w_mem_o"][0], 2 * P)
            keys_and_values(0, 0)
            for h in range(MH):
                keys(1, h)
            with k.turns(sp_, "xattn", B - 2) as b:
                keys_and_values(b + 2, b + 1)
            for h in range(MH):
                values(B - 1, h)
            sc = a["state_ffn_conv"][0].rearrange("b j f -> (b j) f")
            wait(sp_, S.mo_split, 2)
            sp_.dma_start(crow[0:16, :], sc[:, 0:CPART * P]).then_inc(S.conv_in, 16)
            sp_.dma_start(crow1[:], sc[:, CPART * P:FF]).then_inc(S.conv_in, 16)
            with k.turns(sp_, "memo", 3) as i:
                for s in range(2):
                    load(a["w_mem_o"][0], i * (4 * P) + (2 + s) * 2 * P)

            def load_up(j):
                s = begin_load()
                for half, col in ((0, 0), (1, FF)):
                    sp_.dma_start(raw[s][:, :, half * P:half * P + P], rows_of(w_up)[:, :, ds(j * P + col, P)]).then_inc(landed[s], 16)


            for g, (j0, nk) in enumerate(GROUPS):
                with k.turns(sp_, f"up{g}", nk // 2) as i:
                    for s in range(2):
                        load_up(i * 2 + (j0 + s))
                if nk % 2:
                    load_up(j0 + nk - 1)
                with k.turns(sp_, f"down{g}", 4) as i:
                    for s in range(2):
                        load(a["w_ffn_down"][0][j0 * P:(j0 + nk) * P], i * (4 * P) + s * 2 * P, nk)

            n = 0
            for t4 in range(4):
                for blk in range(3):
                    n += 1
                    wait(sp_, S.y_copied, n)
                    cols = slice(t4 * 4 * P, (t4 + 1) * 4 * P)
                    if blk < 2:
                        sp_.dma_start(out["y_p"][0, blk * P:(blk + 1) * P, cols], ytok[:, blk, cols]).then_inc(S.y_out, 16)
                    else:
                        sp_.dma_start(out["y_s"].rearrange("b l d -> (b l) d")[:, cols], ytok[0:NS, 2, cols]).then_inc(S.y_out, 16)
            sp_.wait_ge(S.y_out, 16 * 12)
            sp_.wait_ge(S.conv_out, 64)
            sp_.wait_ge(S.pstate_out, 16 * (GH + HH // 2))
            for s in range(4):
                sp_.wait_ge(s0_out[s], k.now(f"s0_out{s}", 0, 16))
            for s in range(2):
                sp_.wait_ge(mem_out[s], 8 * 16)

        @block.gpsimd
        def _(pool):
            pool.memset(parrow[:], 0.0).then_inc(S.rows_cleared, 1)
            pool.memset(ident[:], 0.0).then_inc(S.made, 1)
            pool.memset(ones[:], 1.0).then_inc(S.made, 1)
            pool.memset(causal[:], 1.0).then_inc(S.made, 1)
            pool.memset(causal8[:], 1.0).then_inc(S.made, 1)
            pool.memset(own8[:], 1.0).then_inc(S.made, 1)
            pool.memset(keep[:], 1.0).then_inc(S.made, 1)
            pool.wait_ge(S.made, 6)
            pool.affine_select(out=ident[:], in_=ident[:], compare_op=ALU.not_equal, fill=1.0, base=0,
                               pattern=[[-1, P]], channel_multiplier=1).then_inc(S.made, 1)
            v = causal[:].rearrange("p (n c) -> p n c", c=C)
            pool.affine_select(out=v, in_=v, compare_op=ALU.is_ge, fill=0.0, base=0,
                               pattern=[[C, CPB], [1, C]], channel_multiplier=-1).then_inc(S.made, 1)
            v8 = causal8[:].rearrange("p (n c) -> p n c", c=L)
            pool.affine_select(out=v8, in_=v8, compare_op=ALU.is_ge, fill=0.0, base=0,
                               pattern=[[L, B], [1, L]], channel_multiplier=-1).then_inc(S.made, 1)
            pool.affine_select(out=own8[:], in_=own8[:], compare_op=ALU.is_ge, fill=0.0, base=0,
                               pattern=[[-L, B]], channel_multiplier=1).then_inc(S.made, 1)
            pool.memset(keep[:, 0:NP:C], 0.0).then_inc(S.made, 1)
            pool.memset(keep[:, NP:NT:L], 0.0).then_inc(S.made, 1)
            pool.wait_ge(S.made, 12)
            pool.affine_select(out=v, in_=v, compare_op=ALU.is_ge, fill=0.0, base=0,
                               pattern=[[-C, CPB], [0, C]], channel_multiplier=1).then_inc(S.made, 1)
            pool.affine_select(out=v8, in_=v8, compare_op=ALU.is_ge, fill=0.0, base=0,
                               pattern=[[-L, B], [0, L]], channel_multiplier=1).then_inc(S.made, 1)
            pool.affine_select(out=own8[:], in_=own8[:], compare_op=ALU.is_ge, fill=0.0, base=L - 1,
                               pattern=[[L, B]], channel_multiplier=-1).then_inc(S.made, 1)
            k = Counts("pool")
            with k.turns(pool, "split", NTILES // 4):
                for t in range(4):
                    wait(pool, high_ready, k.next("tile"))
                    half = raw[t // 2][:, :, (t % 2) * P:(t % 2) * P + P]
                    pool.tensor_tensor(wL[t % 2][:], half, wH[t % 2][:].bitcast(F32), ALU.subtract).then_inc(low_ready, 1)
            for t in range(NTILES % 4):
                wait(pool, high_ready, k.next("tile"))
                half = raw[t // 2][:, :, (t % 2) * P:(t % 2) * P + P]
                pool.tensor_tensor(wL[t % 2][:], half, wH[t % 2][:].bitcast(F32), ALU.subtract).then_inc(low_ready, 1)

        @block.tensor
        def _(pe):
            k = Counts("pe")

            def begin_tile():
                s = k.slot("tile", 2)
                wait(pe, bank_free[s], k.rounds("tile", 2))
                k.add("tile")
                wait(pe, high_ready, k.now("tile"))
                return s

            def tile(nk=KT, mov=(hH, hL), ready=None, extra=None, done=1, cols=NT, work=()):
                s = begin_tile()
                dst = PB[s][:, 0:cols]
                work = sorted(work, key=lambda w: w[0])

                def between(place):
                    while work and work[0][0] <= place:
                        work.pop(0)[1]()

                for t in range(nk):
                    between(2 * t)
                    if ready and t % 4 == 0:
                        wait(pe, ready[0], ready[1] + t // 4)
                    pe.matmul(dst, wH[s][:, t, :], mov[0][:, t, :], start=(t == 0), stop=False)
                    pe.matmul(dst, wH[s][:, t, :], mov[1][:, t, :], start=False, stop=False)
                wait(pe, low_ready, k.now("tile", 1 - done))
                if extra:
                    extra(s)
                for t in range(nk):
                    between(2 * nk + t)
                    mm = pe.matmul(dst, wL[s][:, t, :], mov[0][:, t, :], start=False, stop=(t == nk - 1))
                if done == 2:
                    k.add("tile")
                mm.then_inc(tile_done, done)

            def memory_turn(t):
                wait(pe, bank_free[t % 2], k.rounds("memturn", 2, more=1))
                wait(pe, S.mem_copied, k.now("memturn", min(t, 1)))
                for b in range(2):
                    mm = pe.transpose(T[t % 2][:, b * P:(b + 1) * P], memf[t % 2][:, b * P:(b + 1) * P], ident[:])
                mm.then_inc(S.mem_turned, 1)
                k.add("memturn")

            def memory_tiles(name):
                def four(first):
                    for t in range(4):
                        turn = [(24, lambda t=t: memory_turn((t - 1) % 4))] if t or not first else []
                        tile(mov=(mH, mL), cols=M, work=turn)
                four(True)
                with k.turns(pe, name, 3):
                    four(False)

            pe.wait_ge(S.made, 15)
            pe.wait_ge(S.par_in, 16 * len(PAR))
            for blk in range(PBLK):
                mm = pe.transpose(T[0][:, blk * P:(blk + 1) * P], parrow[:, blk, :], ident[:])
            mm.then_inc(S.par_turned, 1)
            pe.wait_ge(S.mem_in, 16)
            rnd = 0
            for r in range(KT // 2):
                if rnd >= 4:
                    pe.wait_ge(S.tok_low, rnd - 3)
                for t in range(2):
                    for b in range(2):
                        mm = pe.transpose(RB[rnd % 4][:, t * M + b * P:t * M + (b + 1) * P], mtok[:, b, (2 * r + t) * P:(2 * r + t + 1) * P], ident[:])
                mm.then_inc(S.tok_turned, 1)
                rnd += 1
            pe.wait_ge(S.tok_low, rnd)
            memory_tiles("mem_k")
            pe.wait_ge(S.tok_scaled, 3)
            for t in range(KT):
                pe.wait_ge(S.tok_low, rnd - 3)
                for b in range(3):
                    n = P if b < 2 else NS
                    mm = pe.transpose(RB[rnd % 4][:, b * P:b * P + n], xtok[0:n, b, t * P:(t + 1) * P], ident[0:n, 0:n])
                mm.then_inc(S.tok_turned, 1)
                rnd += 1
            memory_turn(3)
            memory_tiles("mem_v")
            pe.wait_ge(S.tok_low, rnd)
            tile(done=2, work=[(24, lambda: memory_turn(3))])
            pe.wait_ge(S.mem_copied, 2 * KT)

            def turn_round(srcs, first=False):
                r = k.slot("turned", 2)
                wait(pe, S.turn_copied, k.now("turned", 0 if first else 1))
                for b in range(3):
                    n = P if b < 2 else NS
                    mm = pe.transpose(T[r][0:n, b * P:(b + 1) * P], srcs[:, b * P:b * P + n], ident[:])
                mm.then_inc(S.turned, 1)
                k.add("turned")

            def tile_copied(back):
                s = (k.n["tile"] - 1 - back) % 2
                wait(pe, bank_free[s], k.rounds("tile", 2, 1 + back, more=1))

            def scores(heads, nk):
                for j in range(heads):
                    for c0, n in ((0, P), (P, P), (NP, NS)):
                        for t in range(nk):
                            u = j if heads == 2 else t
                            mm = pe.matmul(KV[j][0:n, c0:c0 + n], ki[:, u, c0:c0 + n], qd[:, u, c0:c0 + n], start=(t == 0), stop=(t == nk - 1))
                mm.then_inc(S.scores_done, 1)

            def kv_mm(u, rows, blk, keys, wide, kind, n):
                other = {"state_ready": "sample_ready", "sample_ready": "state_ready"}[kind]
                if n == 0:
                    wait(pe, getsem[other], k.now(other))
                elif n > 1:
                    wait(pe, getsem[kind], k.now(kind, 3))
                col = 0 if wide == GV else u * P
                pe.matmul(kv_bank(n, u)[:, 0:wide], keys, vtok[rows, blk, col:col + wide], start=True, stop=True).then_inc(S.kv_done, 1)
                k.add(kind)

            getsem = {"state_ready": S.state_ready, "sample_ready": S.sample_ready}

            def inter(n, heads, blk):
                for j in range(heads):
                    nv, nk = (1, 1) if heads == 2 else (4, 2)
                    for v in range(nv):
                        for t in range(nk):
                            u = j if heads == 2 else t
                            dst = O[j][:, n * C:(n + 1) * C] if heads == 2 else O[blk][:, v * P + n % CPB * C:v * P + n % CPB * C + C]
                            last = n % CPB == CPB - 1 and v == nv - 1 and t == nk - 1
                            mm = pe.matmul(dst, sp[n % 2][:, u, v * P:(v + 1) * P], qi[:, u, n * C:(n + 1) * C],
                                           start=False, stop=last and heads == 1, skip_group_check=True)
                mm.then_inc(S.inter_done, 1)

            def chunk(n, heads, place, gap):
                blk, i = n // CPB, n % CPB
                rows = slice(i * C, (i + 1) * C)

                def product():
                    for u in range(2):
                        kv_mm(u, rows, blk, ktok[rows, blk, u * P:(u + 1) * P], GV if heads == 1 else P, "state_ready", n)

                def queries():
                    wait(pe, S.state_ready, k.now("state_ready", 2))
                    inter(n, heads, blk)
                return [(place, product)] + ([(place + gap, queries)] if n else [])

            def sample(bs, heads):
                for b in bs:
                    s = b % 4 if heads == 1 else k.slot("pair", 2)
                    c0 = NP + b * L
                    for j in range(heads):
                        nv, nk = (1, 1) if heads == 2 else (4, 2)
                        for v in range(nv):
                            for t in range(nk):
                                u = j if heads == 2 else t
                                st = s0h[s][:, b, u, :] if heads == 2 else s0g[s][:, t, v * P:(v + 1) * P]
                                dst = O[j][:, c0:c0 + L] if heads == 2 else O[0][:, v * NS + b * L:v * NS + (b + 1) * L]
                                mm = pe.matmul(dst, st, qd[:, u, c0:c0 + L], start=False, stop=(b == B - 1), skip_group_check=True)
                    if b == B - 1:
                        mm.then_inc(S.o_done, 1)
                    for u in range(2):
                        kv_mm(u, slice(0, NS), 2, kmask[:, b, u * P:(u + 1) * P], GV if heads == 1 else P, "sample_ready", b)

            def intra_gla(blk):
                for v in range(4):
                    pe.matmul(O[blk][:, v * P:(v + 1) * P], vtok[:, blk, v * P:(v + 1) * P], bd[:, 0, blk * P:(blk + 1) * P],
                              start=(v == 0), stop=False, skip_group_check=True)

            tile_copied(0)
            tile_copied(1)
            def decay_logits():
                wait(pe, S.wa_in, k.next("wa", 16))
                wait(pe, S.turn_copied, k.now("turned"))
                wait(pe, S.sample_ready, k.now("sample_ready"))
                wait(pe, S.alog_used, k.now("prep", 0, 2))
                for j in range(2):
                    pe.matmul(T[j][:, 0:NT], wah[:, j * P:(j + 1) * P], gaT[:], start=True, stop=True).then_inc(S.alog_done, 1)

            def turn_keys_first():
                wait(pe, S.prep_ready, k.now("prep"))
                wait(pe, S.sample_ready, k.now("sample_ready"))
                turn_round(ke[:, 0], True)

            def turn_last(v):
                tile_copied(1)
                turn_round(vo[:, v])

            def score_work(heads):
                wait(pe, S.sample_ready, k.now("sample_ready"))
                scores(heads, 3 - heads)

            def outputs_free():
                wait(pe, S.turn_copied, k.now("turned"))
                wait(pe, S.scores_kept, k.now("prep"))
                wait(pe, S.o_copied, k.now("o"))
                wait(pe, S.ss_used, k.now("ss"))

            def gla_first():
                outputs_free()
                intra_gla(0)

            def gla_samples_first():
                k.add("o", 2)
                wait(pe, S.kmask_ready, k.now("prep"))
                wait(pe, S.o_copied, k.now("o", 1))
                for v in range(4):
                    pe.matmul(O[0][:, v * NS:(v + 1) * NS], vtok[0:NS, 2, v * P:(v + 1) * P], bds[:, 0, :],
                              start=(v == 0), stop=False, skip_group_check=True)

            def gla_sample(b):
                wait(pe, s0_in[b % 4], k.next(f"s0_in{b % 4}", 16))
                sample([b], 1)
                if b == B - 1:
                    k.add("o")

            def gla_norm():
                wait(pe, S.squares_ready, k.now("prep"))
                for v in range(4):
                    mm = pe.matmul(O[1][:, 0:NT], ones[:], sqg[:, v, :], start=(v == 0), stop=(v == 3))
                mm.then_inc(S.ss_done, 1)
                k.add("ss")

            with k.turns(pe, "gla", GH) as h:
                tile()
                tile()
                tile(work=[(4, decay_logits)])
                for t in range(3):
                    tile()
                k.add("prep")
                tile(work=[(8, turn_keys_first), (22, lambda: turn_round(ke[:, 1]))])
                tile(work=[(4, lambda: turn_round(vo[:, 0])), (18, lambda: turn_round(vo[:, 1])), (34, lambda: turn_last(2))])
                tile(work=[(12, lambda: turn_last(3)), (26, lambda: score_work(1))])
                tile(work=[(4, gla_first)] + chunk(0, 1, 6, 6) + chunk(1, 1, 18, 6) + chunk(2, 1, 32, 6))
                tile(work=chunk(3, 1, 2, 6) + [(16, lambda: intra_gla(1))] + chunk(4, 1, 18, 6) + chunk(5, 1, 32, 6))
                tile(work=chunk(6, 1, 2, 6) + chunk(7, 1, 16, 6) + [(30, gla_samples_first), (34, lambda: gla_sample(0))])
                tile(work=[(4, lambda: gla_sample(1)), (18, lambda: gla_sample(2)), (32, lambda: gla_sample(3))])
                tile()
                tile(work=[(10, lambda: gla_sample(4)), (32, lambda: gla_sample(5))])
                tile(work=[(2, lambda: gla_sample(6)), (16, lambda: gla_sample(7)), (42, gla_norm)])

            def pair_first():
                outputs_free()
                for j in range(2):
                    for blk in range(2):
                        pe.matmul(O[j][:, blk * P:(blk + 1) * P], vtok[:, blk, j * P:(j + 1) * P], bd[:, j, blk * P:(blk + 1) * P],
                                  start=(blk == 0), stop=False, skip_group_check=True)
                    pe.matmul(O[j][:, NP:NT], vtok[0:NS, 2, j * P:(j + 1) * P], bds[:, j, :], start=False, stop=False, skip_group_check=True)

            def pair_samples_first():
                wait(pe, S.kmask_ready, k.now("prep"))
                sub = k.slot("pair", 2)
                k.add(f"s0_in{sub}", 2)
                wait(pe, s0_in[sub], k.now(f"s0_in{sub}", 0, 16))

            def pair_norm():
                wait(pe, S.squares_ready, k.now("prep"))
                for j in range(2):
                    mm = pe.matmul(O[j][:, 0:NT], ones[:], sqg[:, j, :], start=True, stop=True)
                mm.then_inc(S.ss_done, 1)
                k.add("ss")

            def hgrn_pair():
                for t in range(6):
                    tile()
                k.add("prep")
                tile(work=[(6, turn_keys_first), (14, lambda: turn_round(ke[:, 1])), (22, lambda: score_work(2)),
                           (32, lambda: turn_round(vo[:, 0])), (40, lambda: turn_last(1))])
                tile(work=[(15, pair_first)] + [w for n in range(NC) for w in chunk(n, 2, 16 + 4 * n, 3)])
                tile(work=[(13, pair_samples_first)] + [(14 + 4 * b, lambda b=b: sample([b], 2)) for b in range(B)])
                k.add("o", 2)
                k.add("pair")
                tile(work=[(30, pair_norm)])

            with k.turns(pe, "hgrn", HH // 4):
                hgrn_pair()
                hgrn_pair()

            def residual(s):
                x_slot = k.slot("xst", 2)
                wait(pe, S.xst_ready, k.next("xst"))
                for b in range(3):
                    n = P if b < 2 else NS
                    pe.matmul(PB[s][:, b * P:b * P + n], xst[x_slot][0:n, b, :], ident[0:n, 0:n],
                              start=False, stop=False, skip_group_check=True)

            with k.turns(pe, "wout", 4):
                for t in range(4):
                    tile(ready=(S.mix_split, 1), extra=residual)

            def sum_squares(n):
                pe.wait_ge(S.acc_ready, n)
                pe.matmul(T[0][:, 0:NT], ones[:], acc[:], start=True, stop=True).then_inc(S.sum_done, 1)
            sum_squares(1)
            with k.turns(pe, "memq", 4):
                for t in range(4):
                    tile(ready=(S.normed, 1))

            def turn_keys(h):
                wait(pe, kc_in[h], k.next(f"kc{h}", 16))
                for r in range(2):
                    wait(pe, (S.kT_even, S.kT_odd)[r], k.now("kturn"))
                    for dt in range(2):
                        for mt in range(2):
                            mm = pe.transpose(PB[r][:, dt * M + mt * P:dt * M + (mt + 1) * P],
                                              kc[:, h, mt, (2 * r + dt) * P:(2 * r + dt + 1) * P], ident[:])
                    mm.then_inc(S.k_turned, 1)
                k.add("kturn")

            def keys_copied(back=0):
                wait(pe, S.kT_even, k.now("kturn", back))
                wait(pe, S.kT_odd, k.now("kturn", back))

            def prompt_scores(h):
                keys_copied(0 if h == MH - 1 else 1)
                if h >= 2:
                    pe.wait_ge(S.ppT_copied, h - 1)
                for lt in range(2):
                    for dt in range(4):
                        mm = pe.matmul(T[h % 2][:, lt * M:(lt + 1) * M], q[:, 4 * h + dt, lt * P:(lt + 1) * P], kT[:, h % 2, dt, :],
                                       start=(dt == 0), stop=(dt == 3))
                mm.then_inc(S.sp_done, 1)

            def prompt_values(h):
                pe.wait_ge(S.pp_ready, h + 1)
                for lt in range(2):
                    for mt in range(2):
                        mm = pe.transpose(T[h % 2][:, mt * NP + lt * P:mt * NP + (lt + 1) * P], pP[h % 2][:, lt, mt * P:(mt + 1) * P], ident[:])
                mm.then_inc(S.ppT_done, 1)
                pe.wait_ge(S.ppT_copied, h + 1)
                wait(pe, vc_in[h], k.next(f"vc{h}", 16))
                for dt in range(4):
                    n = 4 * h + dt
                    if n >= 4:
                        pe.wait_ge(S.mop_split, n - 3)
                    for mt in range(2):
                        mm = pe.matmul(RB[n % 4][:, 0:NP], vc[:, h, mt, dt * P:(dt + 1) * P], pTP[h % 2][:, mt, :], start=(mt == 0), stop=(mt == 1))
                    mm.then_inc(S.mop_done if dt < 3 else S.v_used, 1)

            pe.wait_ge(bank_free[0], k.now("tile") // 2)
            pe.wait_ge(bank_free[1], k.now("tile") // 2)
            turn_keys(0)
            turn_keys(1)
            prompt_scores(0)
            for h in range(1, MH):
                if h + 1 < MH:
                    turn_keys(h + 1)
                prompt_scores(h)
                prompt_values(h - 1)
            prompt_values(MH - 1)

            def sample_scores(h):
                keys_copied(0 if h == MH - 1 else 1)
                if h == 0:
                    wait(pe, S.qz_ready, k.now("scored", -1))
                    wait(pe, S.p_ready, k.now("scored"))
                for dt in range(4):
                    mm = pe.matmul(T[0][0:32, 0:M], qz[:, 4 * h + dt, :], kT[:, h % 2, dt, :],
                                   start=(h == 0 and dt == 0), stop=(h == MH - 1 and dt == 3), skip_group_check=True)
                if h == MH - 1:
                    mm.then_inc(S.s_done, 1)
                    k.add("scored")

            def sample_probs():
                k.add("smp")
                wait(pe, S.p_ready, k.now("smp"))
                wait(pe, S.pz_written, k.now("smp", 1))
                for mt in range(2):
                    mm = pe.matmul(T[1][:, mt * 32:(mt + 1) * 32], pr[:, mt * P:(mt + 1) * P], ident[0:32, 0:32], start=True, stop=True)
                mm.then_inc(S.pT_done, 1)

            def sample_values(h, last=False):
                if h == 0:
                    wait(pe, S.pz_written, k.now("smp"))
                wait(pe, vc_in[h], k.next(f"vc{h}", 16))
                for mt in range(2):
                    mm = pe.matmul(RB[h][0:NS, :], pz[:, h, mt, :], vc[:, h, mt, :], start=False, stop=last and mt == 1, skip_group_check=True)
                mm.then_inc(S.v_used, 1)

            turn_keys(0)
            for h in range(1, MH):
                turn_keys(h)
                sample_scores(h - 1)
            pe.wait_ge(S.mop_split, 16)
            pe.wait_ge(S.pz_zeroed, 1)
            for h in range(MH):
                pe.matmul(RB[h][0:NS, :], pz[:, h, 0, :], x[:].rearrange("p k n -> p (k n)")[:, 0:MD], start=True, stop=False, skip_group_check=True)
            sample_scores(MH - 1)
            with k.turns(pe, "xattn", B - 1):
                turn_keys(0)
                sample_probs()
                for h in range(1, MH):
                    turn_keys(h)
                    sample_scores(h - 1)
                    sample_values(h - 1)
                sample_scores(MH - 1)
                sample_values(MH - 1)
            sample_probs()
            for h in range(MH):
                sample_values(h, True)
            for t in range(KT):
                if t % 4 == 0:
                    pe.wait_ge(S.rows_kept, t // 4 + 1)
                mm = pe.transpose(PB[t // 8][:, t % 8 * NS:(t % 8 + 1) * NS], mor[:, t * P:(t + 1) * P], ident[0:NS, 0:NS])
                if t % 8 == 7:
                    mm.then_inc(S.mo_turned, 1)
            wait(pe, S.mo_split, 2)
            with k.turns(pe, "memo", 4):
                for t in range(4):
                    tile()
            pe.wait_ge(S.conv_in, 32)
            for part, rows, n in ((0, crow, CPART), (1, crow1, FT - CPART)):
                for j in range(n):
                    mm = pe.transpose(O[part][:, j * 16:(j + 1) * 16], rows[0:16, j * P:(j + 1) * P], ident[0:16, 0:16])
                mm.then_inc(S.conv_turned, 1)
            sum_squares(2)

            def up():
                for t in range(2):
                    tile(ready=(S.normed, 5))

            def history_rows(first, end):
                pe.wait_ge(S.ug_kept, end)
                for j0 in range(first, end, 4):
                    n = j0 // 4
                    if n >= 4:
                        pe.wait_ge(S.crow_copied, n - 3)
                    for j in range(min(4, end - j0)):
                        mm = pe.transpose(RB[n % 4][0:18, j * P:(j + 1) * P], cnew[:, j0 + j, :], ident[:])
                    mm.then_inc(S.crow_turned, 1)

            for g, (j0, nk) in enumerate(GROUPS):
                with k.turns(pe, f"up{g}", nk // 2):
                    up()
                    up()
                if nk % 2:
                    up()
                if g:
                    history_rows(*((0, CPART) if g == 1 else (CPART, FT)))
                with k.turns(pe, f"down{g}", 4):
                    for t in range(4):
                        tile(nk, (aH, aL), ready=(S.act4, 4 * g + 1))
            sum_squares(3)
            n = 0
            for t4 in range(4):
                pe.wait_ge(S.y_normed, t4 + 1)
                for b in range(3):
                    w = P if b < 2 else NS
                    bank = (KV[0], KV[1])[n % 2]
                    if n >= 2:
                        pe.wait_ge(S.y_copied, n - 1)
                    for t in range(4):
                        mm = pe.transpose(bank[0:w, t * P:(t + 1) * P], x[:, 4 * t4 + t, b * P:b * P + w], ident[:])
                    mm.then_inc(S.y_turned, 1)
                    n += 1

        @block.scalar
        def _(act):
            k = Counts("act")

            def own(ins):
                ins.then_inc(S.act_step, 1)
                k.add("step")

            def settle():
                wait(act, S.act_step, k.now("step"))

            def ahead():
                s = k.slot("ahead", 4)
                wait(act, landed[s // 2], k.rounds("ahead", 4, 0, 32, more=1))
                half = raw[s // 2][:, :, (s % 2) * P:(s % 2) * P + P]
                act.activation(wH[s % 2][:], half, ACT.Copy).then_inc(high_ready, 1)
                k.add("ahead")

            def step(more=True):
                s = k.slot("tile", 2)
                wait(act, tile_done, k.next("tile"))
                if more:
                    ahead()
                return s

            def evac(dst, scale=1.0, more=True):
                s = step(more)
                act.activation(dst, PB[s][:, 0:NT], ACT.Copy, scale=scale).then_inc(bank_free[s], 1)

            def root_guess(v, g):
                wait(act, S.mean_ready, k.next("root"))
                own(act.activation(g, v, ACT.Ln))
                settle()
                act.activation(g, g, ACT.Exp, scale=-0.5).then_inc(S.root_ready, 1)

            def squares(b, n):
                wait(act, S.tok_squared, k.now("squared"))
                k.add("squared")
                act.activation(sqtok[0:n, :], (mtok[:, b, :] if b < 2 else xtok[0:n, b - 2, :]), ACT.Square,
                               accum_out=small[0:n, b:b + 1]).then_inc(S.tok_squared, 1)

            act.wait_ge(S.par_turned, 1)
            act.activation(par[:], T[0][:, 0:PBLK * P].rearrange("p (b n) -> p b n", n=P), ACT.Copy).then_inc(S.par_ready, 1)
            act.wait_ge(S.par_ready, 1)
            for r in range(KT // 2):
                act.wait_ge(S.tok_turned, r + 1)
                for t in range(2):
                    ins = act.activation(mH[:, 2 * r + t, :], RB[r % 4][:, t * M:(t + 1) * M], ACT.Identity, scale=pcol("mem", 2 * r + t))
                ins.then_inc(S.tok_high, 1)
            ahead()
            ahead()
            act.wait_ge(S.mem_in, 16)
            act.wait_ge(S.small_cleared, 1)
            squares(0, P)
            squares(1, P)
            root_guess(small[:, 5:7], small[:, 10:12])
            act.wait_ge(S.lb_shifted, 1)
            act.activation(small[:, 32:64], small[:, 32:64], ACT.Exp).then_inc(S.lb_exp, 1)

            def rows_of_memory(dst):
                def rows(col, t):
                    m = t // 2
                    wait(act, S.mem_turned, k.next("memturn"))
                    if t % 2 == 0:
                        wait(act, mem_out[m], k.now(f"memo{m}", 0, 16))
                    for b in range(2):
                        ins = act.activation(memo[m][:, b, (t % 2) * P:(t % 2 + 1) * P], T[t % 2][:, b * P:(b + 1) * P],
                                             ACT.Copy, scale=small[:, 10 + b:11 + b])
                    ins.then_inc(S.mem_copied, 1)
                    if t % 2:
                        wait(act, S.mem_copied, k.now("memturn"))
                        act.dma_start(dst[:, :, ds(col, 2 * P)], memo[m][:]).then_inc(mem_out[m], 16)
                        k.add(f"memo{m}")

                def four(col, first=False):
                    for t in range(4):
                        s = step()
                        act.activation(memf[s][:], PB[s][:, 0:M], ACT.Copy).then_inc(bank_free[s], 1)
                        if t:
                            rows(col + (t - 1) // 2 * 2 * P, t - 1)
                        elif not first:
                            rows(col - 2 * P, 3)
                return rows, four

            act.wait_ge(S.mem_scales, 1)
            rows, four = rows_of_memory(mk_out)
            four(0, True)
            act.wait_ge(S.x_in, 32)
            squares(2, P)
            four(4 * P)
            squares(3, P)
            squares(4, NS)
            four(8 * P)
            root_guess(small[:, 7:10], small[:, 12:15])
            four(12 * P)
            for t in range(KT):
                act.wait_ge(S.tok_turned, KT // 2 + t + 1)
                act.activation(hH[:, t, :], RB[t % 4][:, 0:NT], ACT.Identity, scale=pcol("mix", t)).then_inc(S.tok_high, 1)
            rows(D - 2 * P, 3)
            rows, four = rows_of_memory(mv_out)
            four(0, True)
            with k.turns(act, "mem_v", 3) as i:
                four(i * (4 * P) + 4 * P)
            rows(D - 2 * P, 3)

            s = step()
            step()
            for half in range(2):
                c = slice(half * NT // 2, (half + 1) * NT // 2)
                act.activation(gaT[:, c], PB[s][0:16, c], ACT.Copy).then_inc(bank_free[(s + half) % 2], 1)

            def copy_round(dst, j, nv=1):
                r = k.slot("turned", 2)
                wait(act, S.turned, k.next("turned"))
                c = slice(j * P, (j + 1) * P)
                act.activation(dst[:, 0:2, c], T[r][:, 0:2 * P].rearrange("p (b n) -> p b n", b=2), ACT.Copy)
                act.activation(dst[0:NS, 2, c], T[r][0:NS, 2 * P:3 * P], ACT.Copy).then_inc(S.turn_copied, 1)

            def gate_exp(first=False):
                s = step(more=not first)
                act.activation(ge[s][:], PB[s][:, 0:NT], ACT.Exp, scale=-1.0).then_inc(S.gate_exp, 1)
                if first:
                    ahead()

            def exps():
                wait(act, S.decay_ready, k.next("decay"))
                act.activation(e1[:], cmid[:], ACT.Exp)
                act.activation(e2[:], cmid[:], ACT.Exp, scale=-1.0)
                act.activation(emid[:], cum[:, :, C // 2 - 1:NP:C], ACT.Exp)
                act.activation(elast[:], cum[:, :, C - 1:NP:C], ACT.Exp).then_inc(S.exps_ready, 1)

            with k.turns(act, "gla", GH) as h:
                evac(qd[:, 0, :], GK ** -0.5)
                evac(qd[:, 1, :], GK ** -0.5)
                wait(act, S.mixed, k.now("mix"))
                for j in range(2):
                    wait(act, S.alog_done, k.next("alog"))
                    act.activation(e1[:, j, :], T[j][:, 0:NT], ACT.Abs, bias=pcol("ba", h * 2 + j)).then_inc(S.abs_ready, 1)
                wait(act, S.abs_ready, k.now("alog"))
                own(act.activation(e1[:], e1[:], ACT.Exp, scale=-1.0))
                settle()
                act.activation(e1[:], e1[:], ACT.Ln, bias=ones[:, 0:1]).then_inc(S.ln_ready, 1)
                evac(ki[:, 0, :])
                exps()
                evac(ki[:, 1, :])
                evac(vo[:, 0, :])
                evac(vo[:, 1, :])
                copy_round(ktok, 0)
                copy_round(ktok, 1)
                evac(vo[:, 2, :])
                copy_round(vtok, 0)
                copy_round(vtok, 1)
                copy_round(vtok, 2)
                evac(vo[:, 3, :])
                copy_round(vtok, 3)
                gate_exp()
                gate_exp()
                k.add("inter", CPB - 1)
                wait(act, S.inter_done, k.now("inter"))
                act.activation(vo[:, :, 0:P], O[0][:].rearrange("p (v n) -> p v n", v=4), ACT.Copy).then_inc(S.o_copied, 1)
                gate_exp()
                k.add("inter", CPB)
                wait(act, S.inter_done, k.now("inter"))
                act.activation(vo[:, :, P:NP], O[1][:].rearrange("p (v n) -> p v n", v=4), ACT.Copy).then_inc(S.o_copied, 1)
                for t in range(4):
                    gate_exp()
                wait(act, S.o_done, k.next("o"))
                act.activation(vo[:, :, NP:NT], O[0][:, 0:4 * NS].rearrange("p (v n) -> p v n", v=4), ACT.Copy).then_inc(S.o_copied, 1)
                wait(act, S.o_copied, k.now("o", 0, 3))
                act.activation(sqg[:], vo[:], ACT.Square).then_inc(S.squares_ready, 1)
                gate_exp()
                root_guess(rsg[:, 0, :], sqg[:, 0, :])
                k.add("mix")

            n_gla = 3 * GH

            def hgrn_pair():
                for j in range(2):
                    s = step()
                    if j == 0:
                        wait(act, S.mixed, k.now("mix"))
                    act.activation(e1[:, j, :], PB[s][:, 0:NT], ACT.Exp, scale=-1.0).then_inc(S.f_exp, 1)
                s = step()
                act.activation(e2[:, 0, :], PB[s][:, 0:NT], ACT.Exp, scale=-1.0).then_inc(S.gate_exp, 1)
                wait(act, S.f_ready, k.next("f"))
                act.activation(e1[:], cum[:], ACT.Ln).then_inc(S.ln_ready, 1)
                s = step()
                act.activation(e2[:, 1, :], PB[s][:, 0:NT], ACT.Exp, scale=-1.0).then_inc(S.gate_exp, 1)
                evac(vo[:, 0, :])
                exps()
                evac(vo[:, 1, :])
                copy_round(ktok, 0)
                copy_round(ktok, 1)
                copy_round(vtok, 0)
                copy_round(vtok, 1)
                gate_exp()
                gate_exp()
                wait(act, S.o_done, k.next("o"))
                for j in range(2):
                    act.activation(vo[:, j, :], O[j][:, 0:NT], ACT.Copy).then_inc(S.o_copied, 1)
                    k.add("o_copied")
                wait(act, S.o_copied, k.now("o_copied", -n_gla))
                act.activation(sqg[:, 0:2, :], vo[:, 0:2, :], ACT.Square).then_inc(S.squares_ready, 1)
                gate_exp()
                gate_exp(first=True)
                root_guess(rsg[:], sqg[:, 0:2, :])
                k.add("mix")

            with k.turns(act, "hgrn", HH // 4):
                hgrn_pair()
                hgrn_pair()

            for g in range(4):
                act.wait_ge(S.mixed, GH + HH // 2 - (g < 3))
                act.activation(hH[:, 4 * g:4 * g + 4, :], omix[:, 4 * g:4 * g + 4, :], ACT.Copy).then_inc(S.mix_high, 1)

            def square_tile(i, t, more=True):
                s = step(more)
                wait(act, bank_free[s], k.rounds("tile", 2, 1, more=1))
                act.activation(sq[s][:], x[:, ds(i * 4 + t, 1), :].rearrange("p a n -> p (a n)"), ACT.Square).then_inc(S.sq_ready, 1)

            def norm_high(gained):
                for g in range(4):
                    wait(act, S.gained, k.now("gained") + 4 * g + 4)
                    act.activation(hH[:, 4 * g:4 * g + 4, :], gained[:, 4 * g:4 * g + 4, :], ACT.Copy).then_inc(S.norm_high, 1)
                k.add("gained", KT)
                root_guess(rs[:], sq[0][:])
                ahead()

            def residual_tiles(name, gained):
                with k.turns(act, name, 3) as i:
                    for t in range(4):
                        square_tile(i, t)
                for t in range(4):
                    square_tile(3, t, more=t < 3)
                norm_high(gained)

            residual_tiles("wout", gainedq)
            with k.turns(act, "memq", 4) as i:
                for t in range(4):
                    step()

            def copy_keys(h):
                wait(act, S.k_turned, k.now("kturn", -1))
                act.activation(kT[:, h % 2, 0:2, :], PB[0][:].rearrange("p (t n) -> p t n", t=2), ACT.Copy).then_inc(S.kT_even, 1)
                k.add("kturn", 2)

            def prompt_exp(h):
                act.wait_ge(S.pmax_ready, h + 1)
                for lt in range(2):
                    ins = act.activation(pP[h % 2][:, lt, :], T[h % 2][:, lt * M:(lt + 1) * M], ACT.Exp, bias=small[:, 2 + lt:3 + lt],
                                         accum_out=small[:, 4 + lt:5 + lt])
                ins.then_inc(S.pp_exp, 1)

            def prompt_probs(h):
                act.wait_ge(S.ppT_done, h + 1)
                act.activation(pTP[h % 2][:], T[h % 2][:].rearrange("p (m n) -> p m n", m=2), ACT.Copy).then_inc(S.ppT_copied, 1)

            def prompt_high(h):
                for dt in range(4):
                    act.wait_ge(*((S.mop_done, 3 * h + dt + 1) if dt < 3 else (S.v_used, h + 1)))
                    act.activation(hH[:, 4 * h + dt, 0:NP], RB[dt][:, 0:NP], ACT.Copy).then_inc(S.mop_high, 1)

            copy_keys(0)
            copy_keys(1)
            prompt_exp(0)
            for h in range(MH):
                if h + 2 < MH:
                    copy_keys(h + 2)
                prompt_probs(h)
                if h + 1 < MH:
                    prompt_exp(h + 1)
                prompt_high(h)

            def sample_exp():
                wait(act, S.max_ready, k.next("max"))
                act.activation(pr[:], T[0][0:32, 0:M], ACT.Exp, bias=small[0:32, 9:10], accum_out=small[0:32, 10:11]).then_inc(S.p_exp, 1)

            def sample_probs(cols):
                wait(act, S.pT_done, k.next("smp"))
                wait(act, S.pz_zeroed, k.now("smp"))
                for mt in range(2):
                    ins = act.activation(pz[:, :, mt, cols], T[1][:, mt * 32:(mt + 1) * 32].rearrange("p (h l) -> p h l", h=MH), ACT.Copy)
                ins.then_inc(S.pz_written, 1)

            for h in range(MH):
                copy_keys(h)
            sample_exp()
            with k.turns(act, "xattn", B - 1) as b:
                copy_keys(0)
                sample_probs(ds(b * L, L))
                for h in range(1, MH):
                    copy_keys(h)
                sample_exp()
            sample_probs(slice((B - 1) * L, B * L))
            k.add("v_used", MH * (B + 1))
            for h in range(0, MH, 2):
                wait(act, S.v_used, k.now("v_used", MH - 1 - h))
                act.activation(mor[:, h * MD:(h + 1) * MD], RB[h][0:NS, :], ACT.Copy).then_inc(S.rows_kept, 1)
                act.wait_ge(S.rows_kept, h + 2)
            for g in range(2):
                act.wait_ge(S.mo_turned, g + 1)
                act.activation(hH[:, 8 * g:8 * g + 8, NP:NT], PB[g][:].rearrange("p (t n) -> p t n", n=NS), ACT.Copy).then_inc(S.mo_high, 1)
            residual_tiles("memo", gainedf)

            for part, (j0, n) in enumerate(((0, CPART), (CPART, FT - CPART))):
                act.wait_ge(S.conv_turned, part + 1)
                act.activation(cin[:, j0:j0 + n, :], O[part][:, 0:16 * n].rearrange("p (j n) -> p j n", n=16), ACT.Copy).then_inc(S.conv_cols, 1)
            act.wait_ge(S.conv_cols, 2)

            def up(j, col, js):
                step()
                smp = seq[js][:, 2 + NP:NSEQ].rearrange("p (b n) -> p b n", b=B)
                act.activation(smp[:, :, 0:2], cin[:, ds(j, 1), :].rearrange("p a (b n) -> p (a b) n", b=B), ACT.Copy).then_inc(S.seq_ready, 1)
                wait(act, S.conv_ready, k.next("conv"))
                act.activation(ce[js][:, 0:NCONV], cv[js][:, 0:NCONV], ACT.Exp, scale=-1.0).then_inc(S.ce_ready, 1)
                step()
                wait(act, S.av_ready, k.now("conv"))
                act.activation(aH[:, ds(col, 1), :].rearrange("p a n -> p (a n)"), av[js][:], ACT.Copy).then_inc(S.act_high, 1)

            def history_rows(first, end):
                if first:
                    act.wait_ge(S.conv_out, 32)
                for j0 in range(first, end, 4):
                    w = min(4, end - j0)
                    act.wait_ge(S.crow_turned, j0 // 4 + 1)
                    c = (j0 - first) * P
                    act.activation(crow[0:18, c:c + w * P], RB[j0 // 4 % 4][0:18, 0:w * P], ACT.Copy).then_inc(S.crow_copied, 1)
                act.wait_ge(S.crow_copied, (end + 3) // 4)
                c = slice(first * P, end * P)
                act.dma_start(out["conv_p"][0, 0][:, c], crow[0:2, 0:(end - first) * P]).then_inc(S.conv_out, 16)
                act.dma_start(out["conv_s"][0].rearrange("b j f -> (b j) f")[:, c], crow[2:18, 0:(end - first) * P]).then_inc(S.conv_out, 16)

            for g, (j0, nk) in enumerate(GROUPS):
                with k.turns(act, f"up{g}", nk // 2) as i:
                    up(i * 2 + j0, i * 2, 0)
                    up(i * 2 + (j0 + 1), i * 2 + 1, 1)
                if nk % 2:
                    up(j0 + nk - 1, nk - 1, 0)
                if g:
                    history_rows(*((0, CPART) if g == 1 else (CPART, FT)))
                if g < 2:
                    with k.turns(act, f"down{g}", 4):
                        for t in range(4):
                            step()
                else:
                    with k.turns(act, "down2", 3) as i:
                        for t in range(4):
                            square_tile(i, t)
                    for t in range(4):
                        s = step(more=t < 2)
                        wait(act, bank_free[s], k.rounds("tile", 2, 1, more=1))
                        act.activation(sq[s][:], x[:, 12 + t, :], ACT.Square).then_inc(S.sq_ready, 1)
            root_guess(rs[:], sq[0][:])
            act.wait_ge(S.conv_out, 64)
            n = 0
            for t4 in range(4):
                for b in range(3):
                    w = P if b < 2 else NS
                    n += 1
                    act.wait_ge(S.y_turned, n)
                    act.activation(ytok[0:w, b, t4 * 4 * P:(t4 + 1) * 4 * P], KV[(n - 1) % 2][0:w, :], ACT.Copy).then_inc(S.y_copied, 1)

        @block.vector
        def _(dve):
            k = Counts("dve")

            def own(ins):
                ins.then_inc(S.dve_step, 1)
                k.add("step")

            def settle():
                wait(dve, S.dve_step, k.now("step"))

            def tile():
                s = k.slot("tile", 2)
                wait(dve, tile_done, k.next("tile"))
                return s

            def refine(v, g, tmp):
                wait(dve, S.root_ready, k.next("root"))
                own(dve.scalar_tensor_tensor(tmp, g, -0.5, g, ALU.mult, ALU.mult))
                settle()
                own(dve.tensor_tensor(tmp, tmp, v, ALU.mult))
                settle()
                own(dve.scalar_tensor_tensor(g, tmp, 1.5, g, ALU.add, ALU.mult))
                settle()

            def token_scales(b0, b1):
                for _ in range(b0, b1):
                    wait(dve, S.tok_squared, k.next("sq"))
                dve.tensor_scalar(small[:, 5 + b0:5 + b1], small[:, b0:b1], 1.0 / D, EPS, ALU.mult, ALU.add).then_inc(S.mean_ready, 1)
                refine(small[:, 5 + b0:5 + b1], small[:, 10 + b0:10 + b1], small[:, b0:b1])

            dve.memset(small[:], 1.0).then_inc(S.small_cleared, 1)
            dve.wait_ge(S.par_ready, 1)
            for r in range(KT // 2):
                dve.wait_ge(S.tok_high, r + 1)
                for t in range(2):
                    ins = dve.scalar_tensor_tensor(mL[:, 2 * r + t, :], RB[r % 4][:, t * M:(t + 1) * M], pcol("mem", 2 * r + t),
                                                   mH[:, 2 * r + t, :].bitcast(F32), ALU.mult, ALU.subtract)
                ins.then_inc(S.tok_low, 1)
            token_scales(0, 2)
            dve.tensor_copy(small[:, 10:12], small[:, 10:12]).then_inc(S.mem_scales, 1)
            l0, l1, top = pcol("lb0", 0, KT), pcol("lb1", 0, KT), small[:, 16:32]
            own(dve.tensor_tensor(top, l0, l1, ALU.max))
            settle()
            own(dve.tensor_tensor(small[:, 32:48], l0, top, ALU.subtract))
            dve.tensor_tensor(small[:, 48:64], l1, top, ALU.subtract).then_inc(S.lb_shifted, 1)
            dve.wait_ge(S.lb_exp, 1)
            own(dve.tensor_tensor(top, small[:, 32:48], small[:, 48:64], ALU.add))
            settle()
            own(dve.reciprocal(top, top))
            settle()
            own(dve.tensor_tensor(lb[:], small[:, 32:48], top, ALU.mult))
            settle()
            own(dve.tensor_scalar(oml[:], lb[:], -1.0, 1.0, ALU.mult, ALU.add))
            token_scales(2, 5)
            for b, n in enumerate((P, P, NS)):
                tok = xtok[0:n, b, :]
                dve.tensor_scalar(tok, tok, small[0:n, 12 + b:13 + b], None, ALU.mult).then_inc(S.tok_scaled, 1)
            for t in range(KT):
                dve.wait_ge(S.tok_high, KT // 2 + t + 1)
                dve.scalar_tensor_tensor(hL[:, t, :], RB[t % 4][:, 0:NT], pcol("mix", t), hH[:, t, :].bitcast(F32),
                                         ALU.mult, ALU.subtract).then_inc(S.tok_low, 1)
            k.add("tile", 34)
            for s in range(2):
                dve.wait_ge(mem_out[s], 8 * 16)
            dve.wait_ge(tile_done, 34)
            own(dve.memset(bd[:], 0.0))
            own(dve.memset(bds[:], 0.0))

            def chunks(ap):
                return ap[:, 0:NP].rearrange("p (n c) -> p n c", c=C), ap[:, NP:NT].rearrange("p (n c) -> p n c", c=L)

            def decays():
                for j in range(2):
                    own(dve.tensor_tensor_scan(cum[:, j, :], keep[:], e1[:, j, :], 0.0, ALU.mult, ALU.add))
                settle()
                for j in range(2):
                    c, _ = chunks(cum[:, j, :])
                    o, _ = chunks(cmid[:, j, :])
                    dve.tensor_tensor(o, c, c[:, :, C // 2 - 1:C // 2].to_broadcast([P, NC, C]), ALU.subtract)
                dve.tensor_copy(cmid[:, :, NP:NT], cum[:, :, NP:NT]).then_inc(S.decay_ready, 1)

            def decayed():
                own(dve.tensor_tensor(ki[:], ki[:], e2[:], ALU.mult))
                own(dve.tensor_tensor(qd[:], qd[:], e1[:], ALU.mult))
                settle()
                for j in range(2):
                    kp, ks = chunks(ki[:, j, :])
                    op, os = chunks(ke[:, j, :])
                    ep, es = chunks(e1[:, j, :])
                    dve.tensor_tensor(op, kp, ep[:, :, C - 1:C].to_broadcast([P, NC, C]), ALU.mult)
                    dve.tensor_tensor(os, ks, es[:, :, L - 1:L].to_broadcast([P, B, L]), ALU.mult)
                for j in range(2):
                    qp, _ = chunks(qd[:, j, :])
                    ins = dve.tensor_tensor(qi[:, j, :].rearrange("p (n c) -> p n c", c=C), qp,
                                            emid[:, j, :].rearrange("p (n o) -> p n o", o=1).to_broadcast([P, NC, C]), ALU.mult)
                ins.then_inc(S.prep_ready, 1)

            def own_keys():
                k.add("turned", 2)
                wait(dve, S.turn_copied, k.now("turned"))
                dve.tensor_tensor(kmask[:], ktok[0:NS, 2:3, :].to_broadcast([NS, B, 2 * P]),
                                  own8[:].rearrange("p (b o) -> p b o", o=1).to_broadcast([NS, B, 2 * P]), ALU.mult).then_inc(S.kmask_ready, 1)

            def keep_scores(heads):
                wait(dve, S.scores_done, k.next("scores"))
                dve.memset(small[:, 15:16], 0.0)
                for j in range(heads):
                    for blk in range(2):
                        dve.copy_predicated(bd[:, j, blk * P:(blk + 1) * P], causal[:].bitcast(U32), KV[j][:, blk * P:(blk + 1) * P])
                    ins = dve.copy_predicated(bds[:, j, :], causal8[:].bitcast(U32), KV[j][0:NS, NP:NT])
                ins.then_inc(S.scores_kept, 1)

            def updates(chunk_range, wide):
                for n in chunk_range:
                    for u in range(2):
                        wait(dve, S.kv_done, k.next("kv"))
                        new, old = sp[(n + 1) % 2][:, u, 0:wide], sp[n % 2][:, u, 0:wide]
                        if n == 0:
                            ins = dve.tensor_copy(new, kv_bank(n, u)[:, 0:wide])
                        else:
                            if n > 1:
                                wait(dve, S.inter_done, k.now("inter") + (n - 1))
                            elif u == 0:
                                wait(dve, S.pstate_out, k.now("pstate", 0, 16))
                            wait(dve, S.state_ready, k.now("st", 1))
                            ins = dve.scalar_tensor_tensor(new, old, elast[:, u, n:n + 1], kv_bank(n, u)[:, 0:wide], ALU.mult, ALU.add)
                        ins.then_inc(S.state_ready, 1)
                        k.add("st")

            def sample_updates(bs, heads, slot=None):
                for b in bs:
                    for u in range(2):
                        wait(dve, S.kv_done, k.next("kv"))
                        c = NP + b * L + L - 1
                        state = s0h[slot][:, b, u, :] if heads == 2 else s0g[b % 4][:, u, :]
                        dve.scalar_tensor_tensor(state, state, e1[:, u, c:c + 1], kv_bank(b, u)[:, 0:(P if heads == 2 else GV)],
                                                 ALU.mult, ALU.add).then_inc(S.sample_ready, 1)
                        k.add("sample_ready")

            def sigmoid(buf):
                own(dve.tensor_scalar(buf, buf, 1.0, None, ALU.add))
                settle()
                own(dve.reciprocal(buf, buf))
                settle()

            def silu_gate(v):
                s = tile()
                wait(dve, S.gate_exp, k.next("gate"))
                sigmoid(ge[s][:])
                dve.tensor_tensor(gate[:, v, :], PB[s][:, 0:NT], ge[s][:], ALU.mult).then_inc(bank_free[s], 1)

            def mix_gate(v):
                s = tile()
                wait(dve, S.gate_exp, k.next("gate"))
                own(dve.tensor_scalar(ge[s][:], ge[s][:], 1.0, None, ALU.add))
                settle()
                own(dve.reciprocal(ge[s][:], ge[s][:]))
                settle()
                dve.tensor_tensor(gate[:, v, :], gate[:, v, :], ge[s][:], ALU.mult).then_inc(bank_free[s], 1)

            with k.turns(dve, "gla", GH) as h:
                for j in range(2):
                    wait(dve, S.abs_ready, k.next("abs"))
                    dve.tensor_scalar(cmid[:, j, :], T[j][:, 0:NT], pcol("ba", h * 2 + j), 0.0, ALU.add, ALU.min).then_inc(S.alog_used, 1)
                wait(dve, S.alog_used, k.now("abs"))
                wait(dve, S.ln_ready, k.next("ln"))
                own(dve.tensor_tensor(e1[:], cmid[:], e1[:], ALU.subtract))
                settle()
                own(dve.tensor_scalar(e1[:], e1[:], 1.0 / 16.0, None, ALU.mult))
                settle()
                decays()
                wait(dve, S.exps_ready, k.next("exps"))
                k.add("tile", 4)
                for s in range(2):
                    wait(dve, bank_free[s], k.rounds("tile", 2))
                decayed()
                k.add("tile", 4)
                own_keys()
                keep_scores(1)
                k.add("turned", 4)
                silu_gate(0)
                updates(range(3), GV)
                silu_gate(1)
                updates(range(3, 6), GV)
                silu_gate(2)
                updates(range(6, NC), GV)
                k.add("inter", NC - 1)
                k.add("pstate")
                sample_updates(range(1), 1)
                silu_gate(3)
                sample_updates(range(1, 4), 1)
                mix_gate(0)
                mix_gate(1)
                sample_updates(range(4, 6), 1)
                mix_gate(2)
                sample_updates(range(6, 8), 1)
                wait(dve, S.sample_ready, k.now("sample_ready"))
                wait(dve, S.ss_done, k.next("ss"))
                dve.tensor_scalar(rsg[:, 0, :], O[1][:, 0:NT], 1.0 / GV, EPS, ALU.mult, ALU.add).then_inc(S.ss_used, 1)
                wait(dve, S.ss_used, k.now("ss"))
                dve.tensor_copy(small[:, 15:16], rsg[:, 0, 0:1]).then_inc(S.mean_ready, 1)
                mix_gate(3)
                refine(rsg[:, 0, :], sqg[:, 0, :], tmpg[:, 0, :])
                for v in range(4):
                    own(dve.scalar_tensor_tensor(tmpg[:, v % 2, :], vo[:, v, :], pcol("glan", h * 4 + v), sqg[:, 0, :], ALU.mult, ALU.mult))
                    settle()
                    ins = dve.tensor_tensor(omix[:, ds(h * 4 + v, 1), :].rearrange("p a n -> p (a n)"), tmpg[:, v % 2, :], gate[:, v, :], ALU.mult)
                    if v < 3:
                        own(ins)
                ins.then_inc(S.mixed, 1)
                k.add("mixed")

            def hgrn_pair(pair, sub):
                for j in range(2):
                    s = tile()
                    wait(dve, S.f_exp, k.next("f_exp"))
                    dve.tensor_scalar(e1[:, j, :], e1[:, j, :], 1.0, None, ALU.add).then_inc(bank_free[s], 1)
                    wait(dve, bank_free[s], k.rounds("tile", 2, 1, more=1))
                    own(dve.reciprocal(e1[:, j, :], e1[:, j, :]))
                    settle()
                    own(dve.tensor_scalar(cum[:, j, :], e1[:, j, :], oml[:, ds(pair * 2 + j, 1)], lb[:, ds(pair * 2 + j, 1)], ALU.mult, ALU.add))
                    settle()
                    ins = dve.tensor_scalar(ki[:, j, :], cum[:, j, :], -1.0, 1.0, ALU.mult, ALU.add)
                    if j == 0:
                        own(ins)
                ins.then_inc(S.f_ready, 1)
                k.add("f_ready")

                def query(j):
                    s = tile()
                    wait(dve, S.gate_exp, k.next("gate"))
                    sigmoid(e2[:, j, :])
                    dve.scalar_tensor_tensor(qd[:, j, :], PB[s][:, 0:NT], P ** -0.5, e2[:, j, :], ALU.mult, ALU.mult).then_inc(bank_free[s], 1)
                query(0)
                wait(dve, S.ln_ready, k.next("ln"))

                for j in range(2):
                    own(dve.tensor_tensor_scan(cum[:, j, :], keep[:], e1[:, j, :], 0.0, ALU.mult, ALU.add))
                settle()
                for j in range(2):
                    c, _ = chunks(cum[:, j, :])
                    o, _ = chunks(cmid[:, j, :])
                    own(dve.tensor_tensor(o, c, c[:, :, C // 2 - 1:C // 2].to_broadcast([P, NC, C]), ALU.subtract))
                query(1)
                dve.tensor_copy(cmid[:, :, NP:NT], cum[:, :, NP:NT]).then_inc(S.decay_ready, 1)
                wait(dve, S.exps_ready, k.next("exps"))
                wait(dve, S.f_ready, k.now("f_ready"))
                for s in range(2):
                    wait(dve, bank_free[s], k.rounds("tile", 2))
                decayed()
                k.add("tile", 2)
                own_keys()
                keep_scores(2)
                k.add("turned", 2)
                silu_gate(0)
                updates(range(NC), P)
                k.add("inter", NC - 1)
                k.add("pstate")
                silu_gate(1)
                sample_updates(range(B), 2, sub)
                mix_gate(0)
                wait(dve, S.sample_ready, k.now("sample_ready"))
                wait(dve, S.ss_done, k.next("ss"))
                own(dve.tensor_scalar(rsg[:, 0, :], O[0][:, 0:NT], 1.0 / P, EPS, ALU.mult, ALU.add))
                dve.tensor_scalar(rsg[:, 1, :], O[1][:, 0:NT], 1.0 / P, EPS, ALU.mult, ALU.add).then_inc(S.ss_used, 1)
                wait(dve, S.ss_used, k.now("ss"))
                settle()
                dve.tensor_copy(small[:, 15:16], rsg[:, 0, 0:1]).then_inc(S.mean_ready, 1)
                mix_gate(1)
                refine(rsg[:], sqg[:, 0:2, :], tmpg[:])
                for j in range(2):
                    own(dve.scalar_tensor_tensor(tmpg[:, j, :], vo[:, j, :], pcol("hgn", pair * 2 + j), sqg[:, j, :], ALU.mult, ALU.mult))
                settle()
                own(dve.tensor_tensor(tmpg[:], tmpg[:], gate[:, 0:2, :], ALU.mult))
                settle()
                wait(dve, S.mixed, k.now("mixed"))
                om = omix[:, ds(pair * 2, 2), :]
                dve.tensor_tensor(om, om, tmpg[:], ALU.add).then_inc(S.mixed, 1)
                k.add("mixed")

            with k.turns(dve, "hgrn", HH // 4) as i:
                hgrn_pair(i * 2, 0)
                hgrn_pair(i * 2 + 1, 1)

            for g in range(4):
                c = slice(4 * g, 4 * g + 4)
                dve.wait_ge(S.mix_high, g + 1)
                dve.tensor_tensor(hL[:, c, :], omix[:, c, :], hH[:, c, :].bitcast(F32), ALU.subtract).then_inc(S.mix_split, 1)

            own(dve.memset(acc[:], 0.0))

            def add_square(s):
                wait(dve, S.sq_ready, k.next("sqr"))
                settle()
                own(dve.tensor_tensor(acc[:], acc[:], sq[s][:], ALU.add))

            def residual_tile(i, t, first=False, square=True, gain=None, gained=None):
                s = tile()
                xt = x[:, ds(i * 4 + t, 1), :].rearrange("p a n -> p (a n)")
                if first:
                    dve.tensor_copy(xt, PB[s][:, 0:NT]).then_inc(bank_free[s], 1)
                else:
                    dve.tensor_tensor(xt, xt, PB[s][:, 0:NT], ALU.add).then_inc(bank_free[s], 1)
                if gain:
                    wait(dve, bank_free[s], k.rounds("tile", 2, 1, more=1))
                    dve.tensor_scalar(gained[:, ds(i * 4 + t, 1), :].rearrange("p a n -> p (a n)"), xt, pcol(gain, i * 4 + t), None, ALU.mult).then_inc(S.gained, 1)
                    k.add("gained")
                if square:
                    add_square(s)

            def norm_scale(between=()):
                settle()
                dve.tensor_copy(acc[:], acc[:]).then_inc(S.acc_ready, 1)
                for f in between[:1]:
                    f()
                wait(dve, S.sum_done, k.next("sum"))
                dve.tensor_scalar(rs[:], T[0][:, 0:NT], 1.0 / D, EPS, ALU.mult, ALU.add).then_inc(S.mean_ready, 1)
                for f in between[1:]:
                    f()
                wait(dve, S.root_ready, k.now("root", -1))
                refine(rs[:], sq[0][:], sq[1][:])
                own(dve.memset(acc[:], 0.0))

            def norm_low(gained):
                def low(g):
                    wait(dve, S.norm_high, k.next("norm_high"))
                    wait(dve, S.gained, k.now("gained"))
                    dve.tensor_tensor(hL[:, 4 * g:4 * g + 4, :], gained[:, 4 * g:4 * g + 4, :], hH[:, 4 * g:4 * g + 4, :].bitcast(F32),
                                      ALU.subtract).then_inc(S.normed, 1)

                def rest():
                    for g in range(1, 4):
                        low(g)
                return lambda: low(0), rest

            dve.wait_ge(S.x_in, 64)
            def stage(i, t):
                s = t % 2
                own(dve.tensor_copy(xst[s][:, 0:2, :], xres[:, 0:2, ds((i * 4 + t) * P, P)]))
                dve.tensor_copy(xst[s][0:NS, 2, :], xres[0:NS, 2, ds((i * 4 + t) * P, P)]).then_inc(S.xst_ready, 1)
            stage(0, 0)
            stage(0, 1)
            with k.turns(dve, "wout", 3) as i:
                for t in range(4):
                    residual_tile(i, t, first=True, gain="xat", gained=gainedq)
                    stage(i, t + 2)
            for t in range(4):
                residual_tile(3, t, first=True, gain="xat", gained=gainedq)
                if t < 2:
                    stage(3, t + 2)
            norm_scale(norm_low(gainedq))
            with k.turns(dve, "memq", 4) as i:
                for t in range(4):
                    s = tile()
                    dve.scalar_tensor_tensor(q[:, ds(i * 4 + t, 1), :].rearrange("p a n -> p (a n)"), PB[s][:, 0:NT], MD ** -0.5, sq[0][:],
                                             ALU.mult, ALU.mult).then_inc(bank_free[s], 1)

            def copy_keys(h):
                k.add("kturn", 2)
                wait(dve, S.k_turned, k.now("kturn"))
                dve.tensor_copy(kT[:, h % 2, 2:4, :], PB[1][:].rearrange("p (t n) -> p t n", t=2)).then_inc(S.kT_odd, 1)

            def low_part(dst_h, dst_l, bank, sem):
                dve.tensor_tensor(dst_l, bank, dst_h.bitcast(F32), ALU.subtract).then_inc(sem, 1)

            def prompt_softmax(h):
                dve.wait_ge(S.sp_done, h + 1)
                own(dve.tensor_reduce(small[:, 0:2], T[h % 2][:].rearrange("p (l m) -> p l m", l=2), AX.X, ALU.max))
                settle()
                dve.tensor_scalar(small[:, 2:4], small[:, 0:2], -1.0, None, ALU.mult).then_inc(S.pmax_ready, 1)
                dve.wait_ge(S.pp_exp, h + 1)
                own(dve.reciprocal(small[:, 6:8], small[:, 4:6]))
                settle()
                own(dve.tensor_scalar(pP[h % 2][:, 0, :], pP[h % 2][:, 0, :], small[:, 6:7], None, ALU.mult))
                dve.tensor_scalar(pP[h % 2][:, 1, :], pP[h % 2][:, 1, :], small[:, 7:8], None, ALU.mult).then_inc(S.pp_ready, 1)

            def prompt_low(h):
                for dt in range(4):
                    n = 4 * h + dt
                    dve.wait_ge(S.mop_high, n + 1)
                    low_part(hH[:, n, 0:NP], hL[:, n, 0:NP], RB[dt][:, 0:NP], S.mop_split)

            def queries(cols):
                for h in range(MH):
                    ins = dve.tensor_copy(qz[:, 4 * h:4 * h + 4, h * L:(h + 1) * L], q[:, 4 * h:4 * h + 4, cols])
                    if h < MH - 1:
                        own(ins)
                ins.then_inc(S.qz_ready, 1)
                k.add("queries")

            def sample_softmax():
                wait(dve, S.s_done, k.next("smp"))
                own(dve.tensor_reduce(small[0:32, 8:9], T[0][0:32, 0:M], AX.X, ALU.max))
                settle()
                dve.tensor_scalar(small[0:32, 9:10], small[0:32, 8:9], -1.0, None, ALU.mult).then_inc(S.max_ready, 1)
                wait(dve, S.p_exp, k.now("smp"))
                own(dve.reciprocal(small[0:32, 11:12], small[0:32, 10:11]))
                settle()
                dve.tensor_scalar(pr[:], pr[:], small[0:32, 11:12], None, ALU.mult).then_inc(S.p_ready, 1)

            own(dve.memset(qz[:], 0.0))
            copy_keys(0)
            copy_keys(1)
            prompt_softmax(0)
            for h in range(MH):
                if h + 2 < MH:
                    copy_keys(h + 2)
                if h + 1 < MH:
                    prompt_softmax(h + 1)
                prompt_low(h)
            settle()
            for s in range(2):
                wait(dve, bank_free[s], k.now("tile") // 2)
            queries(slice(NP, NP + L))
            dve.memset(pz[:], 0.0).then_inc(S.pz_zeroed, 1)
            for h in range(MH):
                copy_keys(h)
            sample_softmax()
            k.add("v_used", MH)
            with k.turns(dve, "xattn", B - 1) as b:
                copy_keys(0)
                wait(dve, S.qz_ready, k.now("queries"))
                queries(ds(b * L + (NP + L), L))
                for h in range(1, MH):
                    copy_keys(h)
                sample_softmax()
                k.add("v_used", MH)
                wait(dve, S.v_used, k.now("v_used"))
                own(dve.tensor_copy(pz[:, :, 0, ds(b * L, L)], qz[:, 0:MH, L:2 * L]))
                dve.tensor_copy(pz[:, :, 1, ds(b * L, L)], qz[:, 0:MH, L:2 * L]).then_inc(S.pz_zeroed, 1)
            k.add("v_used", MH)
            for h in range(1, MH, 2):
                dve.wait_ge(S.rows_kept, h)
                wait(dve, S.v_used, k.now("v_used", MH - 1 - h))
                dve.tensor_copy(mor[:, h * MD:(h + 1) * MD], RB[h][0:NS, :]).then_inc(S.rows_kept, 1)
            for g in range(2):
                dve.wait_ge(S.mo_high, g + 1)
                low_part(hH[:, 8 * g:8 * g + 8, NP:NT], hL[:, 8 * g:8 * g + 8, NP:NT], PB[g][:].rearrange("p (t n) -> p t n", n=NS), S.mo_split)
            own(dve.memset(acc[:], 0.0))
            with k.turns(dve, "memo", 4) as i:
                for t in range(4):
                    residual_tile(i, t, gain="ffn", gained=gainedf)
            norm_scale(norm_low(gainedf))

            own(dve.memset(seq[0][:, 0:2], 0.0))
            own(dve.memset(seq[1][:, 0:2], 0.0))
            settle()

            def up(j, col, js, last4):
                s = tile()
                own(dve.tensor_tensor(seq[js][:, 2:2 + NP], PB[s][:, 0:NP], sq[0][:, 0:NP], ALU.mult))
                smp = seq[js][:, 2 + NP:NSEQ].rearrange("p (b n) -> p b n", b=B)
                dve.tensor_tensor(smp[:, :, 2:2 + L], PB[s][:, NP:NT].rearrange("p (b n) -> p b n", b=B),
                                  sq[0][:, NP:NT].rearrange("p (b n) -> p b n", b=B), ALU.mult).then_inc(bank_free[s], 1)
                wait(dve, bank_free[s], k.rounds("tile", 2, 1, more=1))
                settle()
                wait(dve, S.seq_ready, k.next("conv"))
                own(dve.tensor_scalar(cv[js][:, 0:NCONV], seq[js][:, 0:NCONV], pcol("cw0", j), pcol("cb", j), ALU.mult, ALU.add))
                settle()
                own(dve.scalar_tensor_tensor(cv[js][:, 0:NCONV], seq[js][:, 1:1 + NCONV], pcol("cw1", j), cv[js][:, 0:NCONV], ALU.mult, ALU.add))
                settle()
                dve.scalar_tensor_tensor(cv[js][:, 0:NCONV], seq[js][:, 2:2 + NCONV], pcol("cw2", j), cv[js][:, 0:NCONV], ALU.mult, ALU.add).then_inc(S.conv_ready, 1)
                own(dve.tensor_copy(cnew[:, ds(j, 1), 0:2].rearrange("p a n -> p (a n)"), seq[js][:, NP:NP + 2]))
                dve.tensor_copy(cnew[:, ds(j, 1), 2:18].rearrange("p a (b n) -> p (a b) n", b=B), smp[:, :, L:L + 2]).then_inc(S.ug_kept, 1)
                wait(dve, S.ce_ready, k.now("conv"))
                sigmoid(ce[js][:, 0:NCONV])
                own(dve.tensor_tensor(cv[js][:, 0:NCONV], cv[js][:, 0:NCONV], ce[js][:, 0:NCONV], ALU.mult))
                settle()
                own(dve.tensor_tensor(av[js][:, 0:NP], cv[js][:, 0:NP], sq[0][:, 0:NP], ALU.mult))
                csm = cv[js][:, 2 + NP:2 + NP + B * (L + 2)].rearrange("p (b n) -> p b n", b=B)[:, :, 0:L]
                own(dve.tensor_tensor(av[js][:, NP:NT].rearrange("p (b n) -> p b n", b=B), csm,
                                      sq[0][:, NP:NT].rearrange("p (b n) -> p b n", b=B), ALU.mult))
                settle()
                s = tile()
                dve.tensor_tensor(av[js][:], av[js][:], PB[s][:, 0:NT], ALU.mult).then_inc(bank_free[s], 1)
                wait(dve, bank_free[s], k.rounds("tile", 2, 1, more=1))
                dve.tensor_copy(av[js][:, 0:1], av[js][:, 0:1]).then_inc(S.av_ready, 1)
                wait(dve, S.act_high, k.now("conv"))
                aht = aH[:, ds(col, 1), :].rearrange("p a n -> p (a n)")
                alt = aL[:, ds(col, 1), :].rearrange("p a n -> p (a n)")
                ins = dve.tensor_tensor(alt, av[js][:], aht.bitcast(F32), ALU.subtract)
                if last4:
                    ins.then_inc(S.act4, 1)
                else:
                    own(ins)

            for g, (j0, nk) in enumerate(GROUPS):
                with k.turns(dve, f"up{g}", nk // 4) as i:
                    for t in range(4):
                        up(i * 4 + (j0 + t), i * 4 + t, t % 2, t == 3)
                for t in range(nk % 4):
                    up(j0 + nk // 4 * 4 + t, nk // 4 * 4 + t, t % 2, t == nk % 4 - 1)
                with k.turns(dve, f"down{g}", 4) as i:
                    for t in range(4):
                        residual_tile(i, t, square=g == 2)
            norm_scale()
            for g in range(4):
                for t in range(4):
                    ins = dve.scalar_tensor_tensor(x[:, 4 * g + t, :], x[:, 4 * g + t, :], pcol("fin", 4 * g + t), sq[0][:], ALU.mult, ALU.mult)
                ins.then_inc(S.y_normed, 1)


_INS = ["x_prompt", "x_sample", "mem_prompt", "state_gla", "state_hgrn", "state_ffn_conv", "cache_mem_k", "cache_mem_v",
        "norm_mix_g", "w_in", "gla_w_a_up", "gla_b_a", "gla_norm_g", "hgrn_lower_bound", "hgrn_norm_g", "w_out",
        "norm_xattn_g", "norm_mem_g", "w_mem_q", "w_mem_k", "w_mem_v", "w_mem_o", "norm_ffn_g", "w_ffn_up",
        "ffn_conv_w", "ffn_conv_b", "w_ffn_down", "norm_final_g"]
_OUTS = {"y_p": (1, NP, D), "y_s": (B, L, D), "gla_p": (1, 1, GH, GK, GV), "hgrn_p": (1, 1, HH, P, P),
         "conv_p": (1, 1, 2, FF), "mem_k": (1, 1, M, MH, MD), "mem_v": (1, 1, M, MH, MD),
         "gla_s": (1, B, GH, GK, GV), "hgrn_s": (1, B, HH, P, P), "conv_s": (1, B, 2, FF)}


def kernel(**inputs):
    import numpy as _np
    import concourse.bacc as _bacc
    from concourse.bass_utils import run_bass_kernel_spmd as _run

    nc = _bacc.Bacc("TRN2", target_bir_lowering=False, num_devices=1)
    arrays, ins, outs = {}, {}, {}
    for name in _INS:
        arr = _np.ascontiguousarray(inputs[name])
        arrays[f"in_{name}"] = arr
        ins[name] = nc.dram_tensor(f"in_{name}", arr.shape, mybir.dt.from_np(arr.dtype), kind="ExternalInput").ap()
    for name, shape in _OUTS.items():
        outs[name] = nc.dram_tensor(f"out_{name}", shape, F32, kind="ExternalOutput").ap()
    build(nc, ins, outs)
    r = _run(nc, [arrays], core_ids=[0])
    return tuple(r.results[0][f"out_{name}"] for name in _OUTS)
```
